# Optimizing a Trainium2 kernel written in Bass

```python
import math
import jax, jax.numpy as jnp
from jax import lax
import numpy as np

D_MODEL = 1024
BATCH = 1
SEQ = 256
DEPTH = 2

HEAD_DIM = 64
N_HEADS_A = 8
N_HEADS_B = 8
MOBA_BLOCK = 256
MOBA_TOPK = 3
MOBA_QCHUNK = 32
DILATED_PAIRS = ((128, 1), (512, 4), (2048, 16))
BAND_BLOCK = 128
ROPE_THETA = 10000.0

GDN_QK_HEADS = 8
GDN_V_HEADS = 16
GDN_HEAD_DIM = 128
GDN_CONV = 4
GDN_CHUNK = 64

N_EXPERTS = 32
N_GROUPS = 4
EXPERTS_PER_GROUP = N_EXPERTS // N_GROUPS
TOP_K = 2
D_FF_EXPERT = 512
MOE_BLOCK = 256

LN_EPS = 1e-5
NORM_EPS = 1e-6
NEG = -1e30

N_EVEN = (DEPTH + 1) // 2
N_ODD = DEPTH // 2
AB_HEADS = N_HEADS_A + N_HEADS_B
AB_IN = 3 * AB_HEADS * HEAD_DIM
AB_OUT = AB_HEADS * HEAD_DIM
GDN_QK = GDN_QK_HEADS * GDN_HEAD_DIM
GDN_V = GDN_V_HEADS * GDN_HEAD_DIM
GDN_CONV_CH = 2 * GDN_QK + GDN_V
GDN_IN = GDN_CONV_CH + GDN_V + 2 * GDN_V_HEADS
DEEPNORM_ALPHA = (2.0 * DEPTH) ** 0.25
DEEPNORM_BETA = (8.0 * DEPTH) ** -0.25

kernel_name = "moba_dilated_gdn_grouped_moe_deepnorm"

f32 = jnp.float32

def layer_norm(x, g, b):
    xf = x.astype(f32)
    mu = xf.mean(-1, keepdims=True)
    var = jnp.square(xf - mu).mean(-1, keepdims=True)
    return ((xf - mu) * lax.rsqrt(var + LN_EPS) * g.astype(f32) + b.astype(f32)).astype(x.dtype)

def rope_tables(seq_len, dim):
    inv = ROPE_THETA ** (-jnp.arange(0, dim, 2, dtype=f32) / dim)
    ang = jnp.arange(seq_len, dtype=f32)[:, None] * inv[None, :]
    return jnp.cos(ang), jnp.sin(ang)

def apply_rope(x, cos, sin):
    x1, x2 = jnp.split(x.astype(f32), 2, axis=-1)
    return jnp.concatenate([x1 * cos - x2 * sin, x2 * cos + x1 * sin], -1).astype(x.dtype)

def moba_attention(q, k, v):
    bsz, nh, seq, dh = q.shape
    nblk = -(-seq // MOBA_BLOCK)
    s_pad = nblk * MOBA_BLOCK
    pad = ((0, 0), (0, 0), (0, s_pad - seq), (0, 0))
    q, k, v = jnp.pad(q, pad), jnp.pad(k, pad), jnp.pad(v, pad)
    scale = dh ** -0.5
    kblk = k.reshape(bsz, nh, nblk, MOBA_BLOCK, dh)
    vblk = v.reshape(bsz, nh, nblk, MOBA_BLOCK, dh)
    kmean = kblk.astype(f32).mean(3)
    qblk = jnp.arange(s_pad) // MOBA_BLOCK
    gate = jnp.einsum('bhsd,bhnd->bhsn', q.astype(f32), kmean)
    fully_past = jnp.arange(nblk)[None, :] < qblk[:, None]
    gate = jnp.where(fully_past, gate, NEG)
    ksel = min(MOBA_TOPK, nblk)
    _, sel = lax.top_k(gate, ksel)
    valid = sel < qblk[:, None]
    nchunk = s_pad // MOBA_QCHUNK
    bi = jnp.arange(bsz)[:, None, None]
    hi = jnp.arange(nh)[None, :, None]
    n_sel = ksel * MOBA_BLOCK

    def to_chunks(t):
        return jnp.moveaxis(t.reshape(bsz, nh, nchunk, MOBA_QCHUNK, t.shape[-1]), 2, 0)

    def step(args):
        qc, selc, validc, c = args
        q0 = c * MOBA_QCHUNK
        ob = q0 // MOBA_BLOCK
        flat = selc.reshape(bsz, nh, MOBA_QCHUNK * ksel)
        kg = kblk[bi, hi, flat].reshape(bsz, nh, MOBA_QCHUNK, n_sel, dh)
        vg = vblk[bi, hi, flat].reshape(bsz, nh, MOBA_QCHUNK, n_sel, dh)
        s_sel = jnp.einsum('bhqd,bhqkd->bhqk', qc, kg).astype(f32) * scale
        s_sel = jnp.where(jnp.repeat(validc, MOBA_BLOCK, axis=-1), s_sel, NEG)
        kown = lax.dynamic_index_in_dim(kblk, ob, axis=2, keepdims=False)
        vown = lax.dynamic_index_in_dim(vblk, ob, axis=2, keepdims=False)
        s_own = jnp.einsum('bhqd,bhkd->bhqk', qc, kown).astype(f32) * scale
        causal = (ob * MOBA_BLOCK + jnp.arange(MOBA_BLOCK))[None, :] <= (q0 + jnp.arange(MOBA_QCHUNK))[:, None]
        s_own = jnp.where(causal, s_own, NEG)
        p = jax.nn.softmax(jnp.concatenate([s_sel, s_own], -1), axis=-1).astype(v.dtype)
        return (jnp.einsum('bhqk,bhqkd->bhqd', p[..., :n_sel], vg)
                + jnp.einsum('bhqk,bhkd->bhqd', p[..., n_sel:], vown))

    out = lax.map(step, (to_chunks(q), to_chunks(sel), to_chunks(valid), jnp.arange(nchunk)))
    out = jnp.moveaxis(out, 0, 2).reshape(bsz, nh, s_pad, dh)
    return out[:, :, :seq]

def band_attention(q, k, v, reach):
    *lead, seq_len, dh = q.shape
    w = BAND_BLOCK
    n = seq_len // w
    qb = q.reshape(*lead, n, w, dh)
    kb = k.reshape(*lead, n, w, dh)
    vb = v.reshape(*lead, n, w, dh)

    def with_prev(t):
        prev = jnp.concatenate([jnp.zeros_like(t[..., :1, :, :]), t[..., :-1, :, :]], axis=-3)
        return jnp.concatenate([prev, t], axis=-2)

    kc, vc = with_prev(kb), with_prev(vb)
    s = jnp.einsum('...nqd,...nkd->...nqk', qb, kc).astype(f32) * dh ** -0.5
    dist = (w + jnp.arange(w))[:, None] - jnp.arange(2 * w)[None, :]
    allowed = (dist >= 0) & (dist <= reach)
    first = (jnp.arange(n) == 0)[:, None, None] & (jnp.arange(2 * w) < w)[None, None, :]
    s = jnp.where(allowed[None] & ~first, s, NEG)
    m = s.max(-1, keepdims=True)
    e = jnp.exp(s - m)
    l = e.sum(-1, keepdims=True)
    o = jnp.einsum('...nqk,...nkd->...nqd', (e / l).astype(v.dtype), vc)
    lse = (m + jnp.log(l))[..., 0]
    return o.reshape(*lead, seq_len, dh), lse.reshape(*lead, seq_len)

def to_strided(t, dil, padded_len):
    bsz, nh, seq, dh = t.shape
    t = jnp.swapaxes(t.reshape(bsz, nh, seq // dil, dil, dh), 2, 3)
    return jnp.pad(t, ((0, 0), (0, 0), (0, 0), (0, padded_len - seq // dil), (0, 0)))

def dilated_attention(q, k, v):
    bsz, nh, seq, dh = q.shape
    outs, lses = [], []
    for window, dil in DILATED_PAIRS:
        sub_len = seq // dil
        padded_len = -(-sub_len // BAND_BLOCK) * BAND_BLOCK
        o, lse = band_attention(to_strided(q, dil, padded_len), to_strided(k, dil, padded_len),
                                to_strided(v, dil, padded_len), window // dil)
        outs.append(jnp.swapaxes(o[..., :sub_len, :], 2, 3).reshape(bsz, nh, seq, dh))
        lses.append(jnp.swapaxes(lse[..., :sub_len], 2, 3).reshape(bsz, nh, seq))
    wts = jax.nn.softmax(jnp.stack(lses), axis=0)
    return jnp.einsum('gbhs,gbhsd->bhsd', wts.astype(q.dtype), jnp.stack(outs))

def attention_mixer(x, w_in, w_out, cos, sin):
    bsz, seq, _ = x.shape
    h = (x @ w_in).reshape(bsz, seq, 3, AB_HEADS, HEAD_DIM)
    h = jnp.moveaxis(h, 1, 3)
    q = apply_rope(h[:, 0], cos, sin)
    k = apply_rope(h[:, 1], cos, sin)
    v = h[:, 2]
    o_a = moba_attention(q[:, :N_HEADS_A], k[:, :N_HEADS_A], v[:, :N_HEADS_A])
    o_b = dilated_attention(q[:, N_HEADS_A:], k[:, N_HEADS_A:], v[:, N_HEADS_A:])
    o = jnp.concatenate([o_a, o_b], axis=1)
    return jnp.swapaxes(o, 1, 2).reshape(bsz, seq, AB_OUT) @ w_out

def causal_dwconv(x, w):
    width = w.shape[0]
    return lax.conv_general_dilated(x, w[:, None, :].astype(x.dtype), window_strides=(1,),
                                    padding=[(width - 1, 0)], dimension_numbers=('NWC', 'WIO', 'NWC'),
                                    feature_group_count=x.shape[-1])

def l2norm(t):
    return t * lax.rsqrt(jnp.sum(t * t, -1, keepdims=True) + NORM_EPS)

def gated_delta_rule(q, k, v, g, beta):
    bsz, nh, seq, dk = q.shape
    dv = v.shape[-1]
    c = GDN_CHUNK
    n = seq // c
    q = q * dk ** -0.5
    q, k, v = (t.reshape(bsz, nh, n, c, t.shape[-1]) for t in (q, k, v))
    beta = beta.reshape(bsz, nh, n, c)[..., None]
    gc = jnp.cumsum(g.reshape(bsz, nh, n, c), axis=-1)
    ii = jnp.arange(c)
    lower = ii[:, None] >= ii[None, :]
    strict = ii[:, None] > ii[None, :]
    diff = gc[..., :, None] - gc[..., None, :]
    decay = jnp.where(lower, jnp.exp(jnp.where(lower, diff, 0.0)), 0.0)
    kb = k * beta
    l_mat = jnp.where(strict, jnp.einsum('...ik,...jk->...ij', kb, k) * decay, 0.0)
    a_mat = l_mat + jnp.eye(c, dtype=f32)
    rhs = jnp.concatenate([v * beta, kb * jnp.exp(gc)[..., None]], -1)
    sol = lax.linalg.triangular_solve(a_mat, rhs, left_side=True, lower=True, unit_diagonal=True)
    u, w = sol[..., :dv], sol[..., dv:]
    attn = jnp.einsum('...ik,...jk->...ij', q, k) * decay
    q_dec = q * jnp.exp(gc)[..., None]
    k_dec = k * jnp.exp(gc[..., -1:] - gc)[..., None]
    chunk_decay = jnp.exp(gc[..., -1])

    def step(state, xs):
        u_i, w_i, q_i, k_i, a_i, d_i = xs
        v_new = u_i - jnp.einsum('bhck,bhkv->bhcv', w_i, state)
        o_i = jnp.einsum('bhck,bhkv->bhcv', q_i, state) + jnp.einsum('bhcj,bhjv->bhcv', a_i, v_new)
        state = state * d_i[..., None, None] + jnp.einsum('bhck,bhcv->bhkv', k_i, v_new)
        return state, o_i

    xs = tuple(jnp.moveaxis(t, 2, 0) for t in (u, w, q_dec, k_dec, attn, chunk_decay))
    _, o = lax.scan(step, jnp.zeros((bsz, nh, dk, dv), f32), xs)
    return jnp.moveaxis(o, 0, 2).reshape(bsz, nh, seq, dv)

def gdn_mixer(x, w_in, conv_w, a_log, dt_bias, norm_g, w_out):
    bsz, seq, _ = x.shape
    h = x @ w_in
    qkv, z, b, a = jnp.split(h, [GDN_CONV_CH, GDN_CONV_CH + GDN_V, GDN_CONV_CH + GDN_V + GDN_V_HEADS], axis=-1)
    qkv = jax.nn.silu(causal_dwconv(qkv, conv_w))
    q, k, v = jnp.split(qkv, [GDN_QK, 2 * GDN_QK], axis=-1)
    rep = GDN_V_HEADS // GDN_QK_HEADS

    def heads(t, n):
        return jnp.swapaxes(t.astype(f32).reshape(bsz, seq, n, GDN_HEAD_DIM), 1, 2)

    q = jnp.repeat(l2norm(heads(q, GDN_QK_HEADS)), rep, axis=1)
    k = jnp.repeat(l2norm(heads(k, GDN_QK_HEADS)), rep, axis=1)
    v = heads(v, GDN_V_HEADS)
    beta = jnp.swapaxes(jax.nn.sigmoid(b.astype(f32)), 1, 2)
    g = -jnp.exp(a_log.astype(f32)) * jax.nn.softplus(a.astype(f32) + dt_bias.astype(f32))
    g = jnp.swapaxes(g, 1, 2)
    o = jnp.swapaxes(gated_delta_rule(q, k, v, g, beta), 1, 2)
    zf = z.astype(f32).reshape(bsz, seq, GDN_V_HEADS, GDN_HEAD_DIM)
    o = o * lax.rsqrt(jnp.mean(o * o, -1, keepdims=True) + NORM_EPS) * norm_g.astype(f32) * jax.nn.silu(zf)
    return o.reshape(bsz, seq, GDN_V).astype(x.dtype) @ w_out

def moe_ffn(x, router_w, router_bias, w1, w3, w2):
    bsz, seq, d = x.shape
    n_tok = bsz * seq
    xf = x.reshape(n_tok, d)
    scores = jax.nn.sigmoid(xf.astype(f32) @ router_w.astype(f32))
    sel = (scores + router_bias.astype(f32)).reshape(n_tok, N_GROUPS, EXPERTS_PER_GROUP)
    group_score = lax.top_k(sel, TOP_K)[0].sum(-1)
    grp = jnp.argmax(group_score, axis=-1)
    in_grp = jnp.take_along_axis(sel, grp[:, None, None], axis=1)[:, 0]
    _, local = lax.top_k(in_grp, TOP_K)
    expert = grp[:, None] * EXPERTS_PER_GROUP + local
    gate = jnp.take_along_axis(scores, expert, axis=1)
    gate = gate / gate.sum(-1, keepdims=True)
    n_asg = n_tok * TOP_K
    e_flat = expert.reshape(-1)
    tok_flat = jnp.repeat(jnp.arange(n_tok, dtype=jnp.int32), TOP_K)
    g_flat = gate.reshape(-1)
    order = jnp.argsort(e_flat)
    e_sorted = e_flat[order]
    counts = jnp.zeros((N_EXPERTS,), jnp.int32).at[e_flat].add(1)
    padded = (counts + MOE_BLOCK - 1) // MOE_BLOCK * MOE_BLOCK
    pad_end = jnp.cumsum(padded)
    pad_start = pad_end - padded
    cnt_start = jnp.cumsum(counts) - counts
    dest = pad_start[e_sorted] + jnp.arange(n_asg) - cnt_start[e_sorted]
    n_blocks = -(-n_asg // MOE_BLOCK) + N_EXPERTS
    cap = n_blocks * MOE_BLOCK
    slot_tok = jnp.full((cap,), n_tok, jnp.int32).at[dest].set(tok_flat[order])
    slot_gate = jnp.zeros((cap,), f32).at[dest].set(g_flat[order])
    block_expert = jnp.minimum(jnp.searchsorted(pad_end, jnp.arange(n_blocks) * MOE_BLOCK, side='right'),
                               N_EXPERTS - 1)
    x_pad = jnp.concatenate([xf, jnp.zeros((1, d), xf.dtype)], axis=0)
    xs = x_pad[slot_tok].reshape(n_blocks, MOE_BLOCK, d)

    def expert_block(args):
        xb, e = args
        hb = jax.nn.silu(xb @ w1[e]) * (xb @ w3[e])
        return hb @ w2[e]

    ys = lax.map(expert_block, (xs, block_expert)).reshape(cap, d)
    out = jnp.zeros((n_tok + 1, d), f32).at[slot_tok].add(ys.astype(f32) * slot_gate[:, None])
    return out[:n_tok].reshape(bsz, seq, d).astype(x.dtype)

def setup_inputs(seed: int = 0) -> dict:
    key = jax.random.key(seed)
    ks = jax.random.split(key, 20)

    def nrm(k, shape, scale):
        return jax.random.normal(k, shape, f32) * scale

    beta = DEEPNORM_BETA
    dt = jnp.exp(jax.random.uniform(ks[6], (N_ODD, GDN_V_HEADS), f32, math.log(1e-3), math.log(1e-1)))
    return {
        "x": nrm(ks[0], (BATCH, SEQ, D_MODEL), 1.0),
        "ab_w_in": nrm(ks[1], (N_EVEN, D_MODEL, AB_IN), D_MODEL ** -0.5),
        "ab_w_out": nrm(ks[2], (N_EVEN, AB_OUT, D_MODEL), beta * AB_OUT ** -0.5),
        "gdn_w_in": nrm(ks[3], (N_ODD, D_MODEL, GDN_IN), D_MODEL ** -0.5),
        "gdn_conv_w": nrm(ks[4], (N_ODD, GDN_CONV, GDN_CONV_CH), GDN_CONV ** -0.5),
        "gdn_a_log": jnp.log(jax.random.uniform(ks[5], (N_ODD, GDN_V_HEADS), f32, 1.0, 16.0)),
        "gdn_dt_bias": dt + jnp.log(-jnp.expm1(-dt)),
        "gdn_norm_g": 1.0 + nrm(ks[7], (N_ODD, GDN_HEAD_DIM), 0.02),
        "gdn_w_out": nrm(ks[8], (N_ODD, GDN_V, D_MODEL), beta * GDN_V ** -0.5),
        "mix_ln_g": 1.0 + nrm(ks[9], (DEPTH, D_MODEL), 0.02),
        "mix_ln_b": nrm(ks[10], (DEPTH, D_MODEL), 0.02),
        "router_w": nrm(ks[11], (D_MODEL, N_EXPERTS), D_MODEL ** -0.5),
        "router_bias": nrm(ks[12], (N_EXPERTS,), 0.01),
        "moe_w1": nrm(ks[13], (DEPTH, N_EXPERTS, D_MODEL, D_FF_EXPERT), D_MODEL ** -0.5),
        "moe_w3": nrm(ks[14], (DEPTH, N_EXPERTS, D_MODEL, D_FF_EXPERT), D_MODEL ** -0.5),
        "moe_w2": nrm(ks[15], (DEPTH, N_EXPERTS, D_FF_EXPERT, D_MODEL), beta * D_FF_EXPERT ** -0.5),
        "ffn_ln_g": 1.0 + nrm(ks[16], (DEPTH, D_MODEL), 0.02),
        "ffn_ln_b": nrm(ks[17], (DEPTH, D_MODEL), 0.02),
    }

def reference(x, ab_w_in, ab_w_out, gdn_w_in, gdn_conv_w, gdn_a_log, gdn_dt_bias, gdn_norm_g, gdn_w_out,
              mix_ln_g, mix_ln_b, router_w, router_bias, moe_w1, moe_w3, moe_w2, ffn_ln_g, ffn_ln_b):
    seq = x.shape[1]
    cos, sin = rope_tables(seq, HEAD_DIM)
    for layer in range(DEPTH):
        j = layer // 2
        if layer % 2 == 0:
            mix = attention_mixer(x, ab_w_in[j], ab_w_out[j], cos, sin)
        else:
            mix = gdn_mixer(x, gdn_w_in[j], gdn_conv_w[j], gdn_a_log[j], gdn_dt_bias[j], gdn_norm_g[j], gdn_w_out[j])
        x = layer_norm(DEEPNORM_ALPHA * x + mix, mix_ln_g[layer], mix_ln_b[layer])
        ffn = moe_ffn(x, router_w, router_bias, moe_w1[layer], moe_w3[layer], moe_w2[layer])
        x = layer_norm(DEEPNORM_ALPHA * x + ffn, ffn_ln_g[layer], ffn_ln_b[layer])
    return x


_drawn_inputs = setup_inputs


def setup_inputs(seed=0):
    import zlib

    import numpy as np

    out = dict(_drawn_inputs(seed))
    spreads = {}
    factors = {'gdn_norm_g': 8.0}
    for name, (base, spread) in spreads.items():
        noise = np.random.default_rng([zlib.crc32(name.encode()), seed]).standard_normal(out[name].shape)
        drawn = base * np.exp(spread * noise) if base else spread * noise
        out[name] = __import__('jax').numpy.asarray(drawn.astype(out[name].dtype))
    for name, factor in factors.items():
        out[name] = (out[name] * factor).astype(out[name].dtype)
    return out
```

```python
from contextlib import ExitStack

import numpy as np

import concourse.bass as bass
from concourse import mybir

F32 = mybir.dt.float32
BF16 = mybir.dt.bfloat16
I32 = mybir.dt.int32
U32 = mybir.dt.uint32
U8 = mybir.dt.uint8
ALU = mybir.AluOpType
ACT = mybir.ActivationFunctionType
AX = mybir.AxisListType.X

P = 128
D = 1024
SEQ = 256
NT = SEQ // P
DJ = D // P
HALF = 512
ALPHA = (2.0 * 2) ** 0.25
LN_EPS = 1e-5
NEG = -1e30

DH = 64
HEADS = 16
PAIRS = HEADS // 2
ATT_SCALE = DH ** -0.5

GH = 8
C = 64
NC_ = SEQ // C
GD = 128
GDN_SCALE = GD ** -0.5
NORM_EPS = 1e-6
TAPS = 4
QKV_CH = 4096
LEVELS = 6

NE = 32
NG = 4
EG = NE // NG
FF = 512
CAP = 64
PASSES = SEQ // CAP
NIT = PASSES * NE

OWN_HEAD, OWN_STEP = 7, 7

RING = 6
UNIT_ATT = 0
UNIT_MOE0 = UNIT_ATT + 8
UNIT_GDN = UNIT_MOE0 + 3 * NE
UNIT_MOE1 = UNIT_GDN + 16
UNITS = UNIT_MOE1 + 3 * NE

COLS = {}
_at = 0
for _n, _w in (("ident", P), ("ones", P), ("upper", P), ("mask_a", 384), ("mask_b", 384), ("cos", 64), ("sin", 64),
               ("iota", CAP), ("decay_mask", P)):
    COLS[_n] = (_at, _w)
    _at += _w
N_CONST = _at


def tables():
    out = np.zeros((P, N_CONST), np.float32)
    p = np.arange(P)[:, None]

    def put(name, value):
        a, w = COLS[name]
        out[:, a:a + w] = value

    put("ident", p == np.arange(P)[None])
    put("ones", 1.0)
    put("upper", p < np.arange(P)[None])
    dist = np.concatenate([p - np.arange(P)[None], p + P - np.arange(SEQ)[None]], 1)
    put("mask_a", np.where(dist >= 0, 0.0, NEG))
    many = (dist <= 128).astype(int) + (dist % 4 == 0) + (dist % 16 == 0)
    put("mask_b", np.where((dist >= 0) & (many > 0), np.log(np.maximum(many, 1)), NEG))
    inv = 10000.0 ** (-np.arange(0, DH, 2, dtype=np.float32) / np.float32(DH))
    angle = np.arange(SEQ, dtype=np.float32)[:, None] * inv.astype(np.float32)[None]
    angle = angle.reshape(NT, P, DH // 2).transpose(1, 0, 2).reshape(P, NT * DH // 2)
    put("cos", np.cos(angle))
    put("sin", np.sin(angle))
    put("iota", np.arange(CAP)[None])
    q = np.arange(P)[None]
    put("decay_mask", np.where((p // C == q // C) & (p % C <= q % C), 0.0, NEG))
    levels = np.zeros((P, LEVELS, P), np.float32)
    for n in range(LEVELS):
        s = 1 << n
        levels[:, n] = (p // (2 * s) == q // (2 * s)) & (p % (2 * s) >= s) & (q % (2 * s) < s)
    return out, levels.reshape(P, LEVELS * P)


class Own:

    def __init__(self, eng, sem):
        self.eng, self.sem, self.n, self.loop = eng, sem, 0, None

    def __call__(self, ins):
        ins.then_inc(self.sem, 1)
        self.n += 1

    def wait(self):
        self.eng.wait_ge(self.sem, self.n if self.loop is None else self.loop + self.n)

    def link(self, ins):
        self(ins)
        self.wait()


def build(nc, a, out):
    with ExitStack() as ctx:
        def sb(name, shape, dt=F32):
            return ctx.enter_context(nc.sbuf_tensor(name, shape, dt))

        def sem(name):
            return ctx.enter_context(nc.semaphore(name))

        ring = sb("ring", [P, RING, DJ, HALF])
        x = sb("x", [P, NT, D])
        xT = sb("xT", [P, DJ, SEQ])
        y = sb("y", [P, NT, D])
        arena = sb("arena", [P, 72 * 256])
        const = sb("const", [P, N_CONST])
        levels = sb("levels", [P, LEVELS, P], U8)
        upper_b = sb("upper_b", [P, P], BF16)
        ones_b = sb("ones_b", [P, P], BF16)
        zeros_b = sb("zeros_b", [P, P], BF16)
        rw = sb("rw", [P, DJ, NE])
        rbias = sb("rbias", [P, NE])
        stats = sb("stats", [P, NT, 2, 6])
        mv = sb("mv", [P, NT, 2])
        spread = sb("spread", [P, NT, 3])
        eps = sb("eps", [P, 1])
        psum = [ctx.enter_context(nc.psum_tensor(f"bank{i}", [P, HALF], F32)) for i in range(8)]

        def k(name):
            at, w = COLS[name]
            return const[:, at:at + w]

        ident = k("ident")

        def area(kb, shape, dt=F32, size=4):
            n = int(np.prod(shape)) * size // 4
            at = int(kb * 256)
            v = arena[:, at:at + n]
            if dt != F32:
                v = v.bitcast(dt)
            if len(shape) == 1:
                return v
            names = "abcde"[:len(shape)]
            sizes = {n_: s for n_, s in zip(names[1:], shape[1:])}
            return v.rearrange(f"p ({' '.join(names)}) -> p {' '.join(names)}", **sizes)

        lnp = area(48, [2, D])
        levels_in = area(60, [LEVELS, P])
        qkT = area(0, [2, PAIRS, SEQ])
        vtk = area(16, [NT, HEADS * DH])
        oT = area(24, [PAIRS, SEQ])
        qk_tok = area(32, [NT, HALF])
        rot = area(36, [NT, HALF])
        s_sb = area(40, [4, 384])
        pT = area(56, [2, 384])
        neg_max = area(46, [4, NT])
        row_sum = area(46.125, [4, NT])
        xs = area(0, [NT, 3, DJ, P], BF16, 2)
        res = area(60, [NT, D])
        xeT = area(16, [DJ, CAP])
        pick = area(18, [2, NT, CAP], BF16, 2)
        gpick = area(19, [2, NT, 2, CAP])
        gpT = area(21, [2, NT, P])
        eh = area(23, [SEQ])
        hg = area(24, [SEQ])
        hm = area(25, [2, P])
        hT = area(26, [2, 2, CAP])
        y_e = area(27, [HALF])
        pos = area(29, [NT, NIT + 1])
        gate = area(30.25, [NT, NIT + 1])
        lgT = area(32, [SEQ])
        route_at = 33 * 256

        def scratch(shape, dt=F32):
            nonlocal route_at
            n = int(np.prod(shape)) // (2 if dt == BF16 else 1)
            view = area(route_at / 256, shape, dt, 2 if dt == BF16 else 4)
            route_at += n
            return view

        scores = scratch([NT, NE])
        sel = scratch([NT, NE])
        top = scratch([NT, NG, 8])
        gsum = scratch([NT, 8])
        m8 = scratch([NT, 8])
        i8 = scratch([NT, 8], U32)
        goh = scratch([NT, NG])
        t32 = scratch([NT, NE])
        ing = scratch([NT, EG])
        loh = scratch([NT, 2, EG])
        pair = scratch([NT, EG])
        both = scratch([NT, NE])
        both_b = scratch([NT, NE], BF16)
        gs = scratch([NT])
        cnt = scratch([1])
        gq = area(0, [2, GH, SEQ])
        vtok = area(16, [NC_, GH, GD])
        ktok = area(32, [NC_, 4, GD])
        nlt = area(32, [4, NC_, P])
        tri = area(40, [4, NC_, P])
        ty = area(48, [4, NC_, P])
        triT = area(56, [4, NC_, P])
        att = area(64, [4, NC_, P])
        xc = area(32, [2, 2, TAPS - 1 + SEQ])
        cv = area(37, [2, 2, SEQ])
        ce = area(41, [2, 2, SEQ])
        vT = area(45, [2, NC_, 2, C])
        sq = area(49, [2, SEQ])
        rn = area(51, [2, SEQ])
        gT = area(53, [5, SEQ])
        state = y[:, 0, :].rearrange("p (h d) -> p h d", h=8)
        vnew = area(40, [2, GD])
        vdec = area(41, [2, GD])
        rres = area(42, [2, GD])
        oq = area(43, [2, GD])
        goT = area(0, [2 * GH, SEQ])
        zt = area(40, [2, HALF])
        gcol = sb("gcol", [P, 8, NC_ * GH])
        sdec = sb("sdec", [P, GH, NC_, 2])
        cw = sb("cw", [P, P])
        cw_in = area(58, [P])
        wba = area(59, [DJ, 48])
        ab = area(61, [8])
        norm_g = sb("norm_g", [P, GD])
        gcT = sb("gcT", [16, SEQ])
        flag = sb("flag", [P, 2, 2], I32)

        const_in, small_in, x_in, ln_in, gdn_in, out_done = (sem(n) for n in ("const_in", "small_in", "x_in", "ln_in", "gdn_in", "out_done"))
        slot_full = [sem(f"slot_full{i}") for i in range(RING)]
        init = sem("init")
        own_act, own_dve = sem("own_act"), sem("own_dve")
        x_ready = sem("x_ready")
        xT_ps, xT_sb = sem("xT_ps"), sem("xT_sb")
        y_sb, var_sb, rstd_sb = sem("y_sb"), sem("var_sb"), sem("rstd_sb")
        mix_ps = sem("mix_ps")
        proj_ps, rope_sb, v_sb, tr_ps, qkT_sb = (sem(n) for n in ("proj_ps", "rope_sb", "v_sb", "tr_ps", "qkT_sb"))
        s_ps, s_read, max_sb, exp_sb, p_sb = (sem(n) for n in ("s_ps", "s_read", "max_sb", "exp_sb", "p_sb"))
        pT_ps, pT_sb, o_ps, oT_sb = (sem(n) for n in ("pT_ps", "pT_sb", "o_ps", "oT_sb"))
        lgT_ps, lgT_sb, lg_ps, sc_sb, a_sb, rank_ps, pos_sb = (
            sem(n) for n in ("lgT_ps", "lgT_sb", "lg_ps", "sc_sb", "a_sb", "rank_ps", "pos_sb"))
        part_act, left_sb, xs_sb, flag_sb = sem("part_act"), sem("left_sb"), sem("xs_sb"), sem("flag_sb")
        cw_ps, cw_sb = sem("cw_ps"), sem("cw_sb")
        ba_ps, ba_exp, ba_ab, ba_sp, gc_sb, col_ps, col_sb, col_exp = (
            sem(n) for n in ("ba_ps", "ba_exp", "ba_ab", "ba_sp", "gc_sb", "col_ps", "col_sb", "col_exp"))
        cv_ps, xc_sb, cv_sb, ce_sb, si_sb, sq_sb, ss_ps, qk_sb, vt_ps, vt_sb = (
            sem(n) for n in ("cv_ps", "xc_sb", "cv_sb", "ce_sb", "si_sb", "sq_sb", "ss_ps", "qk_sb", "vt_ps", "vt_sb"))
        row_ps, dm_sb, dt_sb, kk_ps, kk_sb = (sem(n) for n in ("row_ps", "dm_sb", "dt_sb", "kk_ps", "kk_sb"))
        ly_ps, ly_sb, tl_ps, tri_sb, tt_ps, tt_sb = (
            sem(n) for n in ("ly_ps", "ly_sb", "tl_ps", "tri_sb", "tt_ps", "tt_sb"))
        kt_ps, kt_sb, ks_ps, r_sb, oq_sb, tr2_ps, vn_sb, vd_sb, ao_ps, ao_sb, su_ps, st_sb = (
            sem(n) for n in ("kt_ps", "kt_sb", "ks_ps", "r_sb", "oq_sb", "tr2_ps", "vn_sb", "vd_sb", "ao_ps", "ao_sb",
                             "su_ps", "st_sb"))
        tri_init, dec_exp = sem("tri_init"), sem("dec_exp")
        ss_sb, rms_sb = sem("ss_sb"), sem("rms_sb")
        z_ps, z_exp, og_sb, gt_ps, gt_sb = (
            sem(n) for n in ("z_ps", "z_exp", "og_sb", "gt_ps", "gt_sb"))

        class Moe:

            def __init__(self, sems, runs=0, experts=0):
                (self.pick,
                 self.gathered,
                 self.xe,
                 self.gpt,
                 self.w1_used,
                 self.h_ps,
                 self.sig,
                 self.hm,
                 self.hT_ps,
                 self.hT,
                 self.y_ps,
                 self.y,
                 self.own,
                 self.scattered,
                 ) = sems
                self.runs, self.e, self.g, self.z = runs, experts, experts + runs, experts + 2 * runs
                self.o = OWN_HEAD * runs + OWN_STEP * experts

        def moe_sems(name):
            return [sem(f"{name}_{s}") for s in ("pick", "gathered", "xe", "gpt", "w1_used", "h_ps", "sig", "hm", "hT_ps",
                                                 "hT", "y_ps", "y", "own", "scattered")]

        fast_sems = moe_sems("moe")
        fast = [Moe(fast_sems), Moe(fast_sems, 1, NE)]
        more = [Moe(moe_sems("more0")), Moe(moe_sems("more1"))]
        more_full = [[sem(f"more{layer}_full{i}") for i in range(RING)] for layer in range(2)]

        block = ctx.enter_context(nc.Block())

        def rows(w, cols):
            return w[:, cols].rearrange("(p j) n -> p j n", j=DJ)

        def tiles(w, cols):
            return w[:, cols].rearrange("(c p) n -> p c n", p=P)

        def expert_parts(layer, e):
            w1 = a["moe_w1"][layer, bass.ds(e, 1)].rearrange("a (p j) f -> (a p) j f", j=DJ)
            w3 = a["moe_w3"][layer, bass.ds(e, 1)].rearrange("a (p j) f -> (a p) j f", j=DJ)
            w2 = a["moe_w2"][layer, bass.ds(e, 1)].rearrange("a (h p c) n -> (a p) h (c n)", h=2, c=2)
            return w1, w3, w2

        def w2_view(slot):
            return ring[:, slot].rearrange("p (h q) n -> p h (q n)", h=2).rearrange("p h (c n) -> p h c n", c=2)

        @block.sync
        def _(sp):
            def consumed(u):
                if u < UNIT_ATT + 6:
                    return proj_ps, 2 * (u - UNIT_ATT) + 2
                if u < UNIT_MOE0:
                    return mix_ps, 4
                if u < UNIT_GDN:
                    n, m = divmod(u - UNIT_MOE0, 3)
                    return (fast[0].w1_used, fast[0].h_ps, fast[0].y_ps)[m], n + 1
                u -= UNIT_GDN
                if u < 8:
                    return cv_ps, 2 * u + 2
                if u < 12:
                    return z_ps, 2 * (u - 8) + 2
                return mix_ps, 12

            def load(u, src):
                if u >= RING:
                    sp.wait_ge(*consumed(u - RING))
                sp.dma_start(ring[:, u % RING], src).then_inc(slot_full[u % RING], 16)

            def part(m, slot):
                dst = ring[:, slot]
                return dst.rearrange("p (h q) n -> p h (q n)", h=2) if m == 2 else dst

            def load_experts(layer, u0):
                s = fast[layer]
                for n in range(2):
                    for m, src in enumerate(expert_parts(layer, n)):
                        u = u0 + 3 * n + m
                        sp.wait_ge(*consumed(u - RING))
                        sp.dma_start(part(m, u % RING), src).then_inc(slot_full[u % RING], 16)
                with sp.Fori(1, NE // 2) as i:
                    for b in range(2):
                        for m, src in enumerate(expert_parts(layer, i * 2 + b)):
                            u = u0 + 3 * b + m
                            sp.wait_ge((s.w1_used, s.h_ps, s.y_ps)[m], i * 2 + (b - 1 + s.e))
                            sp.dma_start(part(m, u % RING), src).then_inc(slot_full[u % RING], 16)

            def load_more(layer):
                s = more[layer]
                sp.wait_ge(flag_sb, layer + 1)
                over = sp.value_load(flag[0:1, layer, 0:1])
                with sp.If(over > CAP):
                    sp.wait_ge(fast[layer].y_ps, NE + fast[layer].e)
                    for n in range(2):
                        for m, src in enumerate(expert_parts(layer, n)):
                            sp.dma_start(part(m, 3 * n + m), src).then_inc(more_full[layer][3 * n + m], 16)
                    with sp.Fori(1, (NIT - NE) // 2) as i:
                        for b in range(2):
                            e = (i * 2 + b) % NE
                            for m, src in enumerate(expert_parts(layer, e)):
                                sp.wait_ge((s.w1_used, s.h_ps, s.y_ps)[m], i * 2 + (b - 1 + s.e))
                                sp.dma_start(part(m, 3 * b + m), src).then_inc(more_full[layer][3 * b + m], 16)
                    sp.wait_ge(s.y_ps, NIT - NE)
                with sp.Else():
                    sp.nop()

            sp.dma_start(x[:], a["x"].rearrange("b (t p) d -> p (b t) d", p=P)).then_inc(x_in, 16)
            sp.dma_start(const[:], a["const"]).then_inc(const_in, 16)
            for g in range(2):
                for w in range(3):
                    load(UNIT_ATT + 3 * g + w, rows(a["ab_w_in"][0], slice(w * D + g * HALF, w * D + (g + 1) * HALF)))
            for h in range(2):
                load(UNIT_ATT + 6 + h, tiles(a["ab_w_out"][0], slice(h * HALF, (h + 1) * HALF)))
            load_experts(0, UNIT_MOE0)
            load_more(0)
            for u in range(12):
                load(UNIT_GDN + u, rows(a["gdn_w_in"][0], slice(u * HALF, (u + 1) * HALF)))
            for h in range(2):
                for g in range(2):
                    load(UNIT_GDN + 12 + 2 * h + g,
                         tiles(a["gdn_w_out"][0][g * D:(g + 1) * D], slice(h * HALF, (h + 1) * HALF)))
            load_experts(1, UNIT_MOE1)
            load_more(1)
            for t in range(NT):
                sp.wait_ge(x_ready, 7 + t)
                sp.dma_start(out[0, t * P:(t + 1) * P, :], x[:, t]).then_inc(out_done, 16)
            sp.wait_ge(out_done, 16 * NT)

        @block.gpsimd
        def _(pool):
            def load_ln(n, g, b):
                pool.dma_start(lnp[:, 0], g.partition_broadcast(P)).then_inc(ln_in, 16)
                pool.dma_start(lnp[:, 1], b.partition_broadcast(P)).then_inc(ln_in, 16)

            def parts(layer):
                for t in range(NT):
                    pool.wait_ge(part_act, 4 * layer + t + 1)
                    nc.gpsimd.tensor_tensor(out=res[:, t].rearrange("p (j q) -> p j q", j=DJ),
                                            in0=x[:, t].rearrange("p (q j) -> p j q", j=DJ), in1=xs[:, t, 0],
                                            op=ALU.subtract).then_inc(left_sb, 1)
                for t in range(NT):
                    pool.wait_ge(part_act, 4 * layer + 2 + t + 1)
                    nc.gpsimd.tensor_tensor(out=xs[:, t, 2], in0=res[:, t].rearrange("p (j q) -> p j q", j=DJ),
                                            in1=xs[:, t, 1], op=ALU.subtract).then_inc(xs_sb, 1)

            nc.gpsimd.memset(zeros_b[:], 0.0).then_inc(init, 1)
            nc.gpsimd.memset(flag[:], 0).then_inc(init, 1)
            nc.gpsimd.memset(eps[:], NORM_EPS).then_inc(init, 1)
            load_ln(0, a["mix_ln_g"][0], a["mix_ln_b"][0])
            pool.dma_start(levels_in, a["levels"].rearrange("p (n q) -> p n q", n=LEVELS)).then_inc(small_in, 16)
            pool.dma_start(rw[:], a["router_w"].rearrange("(p j) e -> p j e", j=DJ)).then_inc(small_in, 16)
            pool.dma_start(rbias[:], a["router_bias"].partition_broadcast(P)).then_inc(small_in, 16)
            pool.dma_start(norm_g[:], a["gdn_norm_g"][0].partition_broadcast(P)).then_inc(small_in, 16)
            pool.wait_ge(x_ready, 2)
            load_ln(1, a["ffn_ln_g"][0], a["ffn_ln_b"][0])
            parts(0)
            pool.wait_ge(x_ready, 4)
            pool.dma_start(cw_in, a["gdn_conv_w"][0].rearrange("w (c p) -> (w c) p", p=P)).then_inc(gdn_in, 16)
            nc.gpsimd.memset(wba, 0.0).then_inc(init, 1)
            pool.wait_ge(init, 4)
            for i, at in enumerate((0, 32)):
                src = a["gdn_w_in"][0][:, QKV_CH + 2048 + 16 * i:QKV_CH + 2048 + 16 * (i + 1)]
                pool.dma_start(wba[:, :, at:at + 16], src.rearrange("(p j) n -> p j n", j=DJ)).then_inc(gdn_in, 16)
            pool.dma_start(ab[32:48, 0:1], a["gdn_dt_bias"].rearrange("o h -> h o")).then_inc(gdn_in, 16)
            pool.dma_start(ab[32:48, 1:2], a["gdn_a_log"].rearrange("o h -> h o")).then_inc(gdn_in, 16)
            for n in range(2):
                nc.gpsimd.memset(xc[:, n, :, 0:TAPS - 1], 0.0).then_inc(init, 1)
            pool.wait_ge(tt_sb, 2 * LEVELS * 4)
            load_ln(2, a["mix_ln_g"][1], a["mix_ln_b"][1])
            pool.wait_ge(x_ready, 6)
            load_ln(3, a["ffn_ln_g"][1], a["ffn_ln_b"][1])
            parts(1)

        @block.tensor
        def _(pe):
            mm, transpose = nc.tensor.matmul, nc.tensor.transpose

            zeros_row = zeros_b[:].unsqueeze(1).to_broadcast([P, 4, P])

            def slot_ready(u):
                pe.wait_ge(slot_full[u % RING], 16 * (u // RING + 1))

            def transpose_x(n):
                for t in range(NT):
                    if n:
                        pe.wait_ge(x_ready, 2 * (n - 1) + 1 + t)
                        pe.wait_ge(mix_ps, 4 * n)
                        pe.wait_ge(y_sb, 2 * n)
                    for b in range(4):
                        for jj in range(2):
                            j = 2 * b + jj
                            last = transpose(psum[b][:, jj * SEQ + t * P:jj * SEQ + (t + 1) * P], x[:, t, j::DJ], ident)
                        if t:
                            last.then_inc(xT_ps, 1)

            def attention():
                pe.wait_ge(x_in, 16)
                pe.wait_ge(const_in, 16)
                transpose_x(0)
                pe.wait_ge(xT_sb, 4)
                order = [(0, 0), (0, 1), (0, 2), (1, 0), (1, 1), (1, 2)]
                qk = [n for n in range(6) if order[n][1] < 2]

                def project(n):
                    u = UNIT_ATT + n
                    slot_ready(u)
                    for t in range(NT):
                        if n:
                            if order[n - 1][1] < 2:
                                pe.wait_ge(rope_sb, 2 * qk.index(n - 1) + t + 1)
                            else:
                                pe.wait_ge(v_sb, 2 * (n // 3 - 1) + t + 1)
                        for j in range(DJ):
                            last = mm(psum[4 + t][:], xT[:, j, t * P:(t + 1) * P], ring[:, u % RING, j],
                                      start=(j == 0), stop=(j == DJ - 1))
                        last.then_inc(proj_ps, 1)

                def transpose_qk(n):
                    i = qk.index(n)
                    for t in range(NT):
                        pe.wait_ge(rope_sb, 2 * i + t + 1)
                        if i:
                            pe.wait_ge(qkT_sb, 2 * (i - 1) + t + 1)
                        for q in range(4):
                            last = transpose(psum[6 + t][:, q * P:(q + 1) * P], qk_tok[:, t, q * P:(q + 1) * P], ident)
                        last.then_inc(tr_ps, 1)

                for n in range(6):
                    project(n)
                    if n and order[n - 1][1] < 2:
                        transpose_qk(n - 1)
                pe.wait_ge(qkT_sb, 8)
                pe.wait_ge(v_sb, 4)

                def scores(h):
                    e, pair, bank = h % 2, h // 2, psum[h % 2]
                    if h >= 2:
                        pe.wait_ge(s_read, h - 1)
                    part = slice(e * DH, (e + 1) * DH)
                    mm(bank[:, 0:P], qkT[part, 0, pair, 0:P], qkT[part, 1, pair, 0:P], start=True, stop=True)
                    mm(bank[:, P:3 * P], qkT[part, 0, pair, P:SEQ], qkT[part, 1, pair, :],
                       start=True, stop=True).then_inc(s_ps, 1)

                def transpose_p(h):
                    pe.wait_ge(p_sb, h + 1)
                    if h >= 2:
                        pe.wait_ge(pT_sb, h - 1)
                    for q in range(3):
                        last = transpose(psum[2 + h % 2][:, q * P:(q + 1) * P], s_sb[:, h % 4, q * P:(q + 1) * P], ident)
                    last.then_inc(pT_ps, 1)

                def values(h):
                    e, pair = h % 2, h // 2
                    pe.wait_ge(pT_sb, h + 1)
                    if pair >= 2:
                        pe.wait_ge(oT_sb, pair - 1)
                    o = psum[4 + pair % 2][e * DH:(e + 1) * DH]
                    col = slice(h * DH, (h + 1) * DH)
                    mm(o[:, 0:SEQ], vtk[:, 0, col], pT[:, h % 2, 0:SEQ], start=True, stop=False)
                    mm(o[:, P:SEQ], vtk[:, 1, col], pT[:, h % 2, SEQ:3 * P], start=False, stop=True).then_inc(o_ps, 1)

                for n in range(HEADS + 3):
                    if n < HEADS:
                        scores(n)
                    if 2 <= n < HEADS + 2:
                        transpose_p(n - 2)
                    if n >= 3:
                        values(n - 3)
                pe.wait_ge(oT_sb, PAIRS)
                for h in range(2):
                    slot_ready(UNIT_ATT + 6 + h)
                for t in range(NT):
                    for h in range(2):
                        u = UNIT_ATT + 6 + h
                        for c in range(PAIRS):
                            last = mm(psum[2 * h + t][:], oT[:, c, t * P:(t + 1) * P], ring[:, u % RING, c],
                                      start=(c == 0), stop=(c == PAIRS - 1))
                        last.then_inc(mix_ps, 1)

            def router(layer):
                pe.wait_ge(small_in, 64)
                transpose_x(1 + 2 * layer)
                pe.wait_ge(xT_sb, 4 * (2 + 2 * layer))
                for j in range(DJ):
                    last = mm(psum[4][0:NE, 0:SEQ], rw[:, j], xT[:, j], start=(j == 0), stop=(j == DJ - 1))
                last.then_inc(lgT_ps, 1)
                pe.wait_ge(init, 2)
                for b in range(4):
                    mm(psum[b][:], zeros_b[:], zeros_row, start=True, stop=False)
                pe.wait_ge(lgT_sb, layer + 1)
                for t in range(NT):
                    last = transpose(psum[5][:, t * NE:(t + 1) * NE], lgT[0:NE, t * P:(t + 1) * P], ident[0:NE, 0:NE])
                last.then_inc(lg_ps, 1)
                pe.wait_ge(a_sb, layer + 1)
                r = psum[6]
                mm(r[:, 0:NE], upper_b[:], both_b[:, 0], start=True, stop=True)
                mm(r[:, NE:2 * NE], ones_b[:], both_b[:, 0], start=True, stop=False)
                mm(r[:, NE:2 * NE], upper_b[:], both_b[:, 1], start=False, stop=True)
                mm(r[:, 2 * NE:3 * NE], ones_b[:], both_b[:, 0], start=True, stop=False)
                mm(r[:, 2 * NE:3 * NE], ones_b[:], both_b[:, 1], start=False, stop=True).then_inc(rank_ps, 1)

            def gather(s, b, wait):
                pe.wait_ge(s.pick, wait + s.g)
                for j in range(DJ):
                    for t in range(NT):
                        for part in range(3):
                            mm(psum[4][:, j * CAP:(j + 1) * CAP], xs[:, t, part, j], pick[:, b, t],
                               start=(t == 0 and part == 0), stop=(t == NT - 1 and part == 2))
                for t in range(NT):
                    last = transpose(psum[5][:, t * P:(t + 1) * P],
                                     gpick[:, b, t].rearrange("p d s -> p (d s)"), ident)
                last.then_inc(s.gathered, 1)

            def scatter(s, b, wait):
                pe.wait_ge(s.y, wait + s.g)
                pe.wait_ge(s.gpt, wait + s.z)
                for t in range(NT):
                    for h in range(2):
                        part = slice(h * CAP, (h + 1) * CAP)
                        last = mm(psum[2 * h + t][:], gpT[part, b, t], y_e[part], start=False, stop=False,
                                  skip_group_check=True)
                return last

            def experts(s, fulls, steps, first):
                gather(s, 0, 1)
                with pe.Fori(0, steps // 2) as i:
                    for b in range(2):
                        n = i * 2 + b
                        slots = [(first + 3 * b + m) % RING for m in range(3)]
                        filled = [i * 16 + 16 * ((first + 3 * b + m) // RING + 1) for m in range(3)]
                        pe.wait_ge(s.xe, n + (1 + s.g))
                        pe.wait_ge(s.gpt, n + (2 + s.z))
                        for m in range(2):
                            pe.wait_ge(fulls[slots[m]], filled[m])
                            for j in range(DJ):
                                for h in range(2):
                                    last = mm(psum[5][h * CAP:(h + 1) * CAP, m * SEQ:(m + 1) * SEQ], xeT[:, j],
                                              ring[:, slots[m], j, h * SEQ:(h + 1) * SEQ],
                                              start=(j == 0), stop=(j == DJ - 1))
                            last.then_inc((s.w1_used, s.h_ps)[m], 1)
                        scatter(s, 1 - b, n + 1)
                        pe.wait_ge(s.hm, n + (1 + s.e))
                        for c in range(2):
                            last = transpose(psum[6][:, c * P:(c + 1) * P], hm[:, c], ident)
                        last.then_inc(s.hT_ps, 1)
                        gather(s, 1 - b, n + 2)
                        pe.wait_ge(s.hT, n + (1 + s.e))
                        pe.wait_ge(fulls[slots[2]], filled[2])
                        w2 = w2_view(slots[2])
                        for g in range(2):
                            for c in range(2):
                                for h in range(2):
                                    last = mm(psum[7][h * CAP:(h + 1) * CAP], hT[:, c, g],
                                              w2[:, g, c, h * HALF:(h + 1) * HALF],
                                              start=(g == 0 and c == 0), stop=(g == 1 and c == 1))
                        last.then_inc(s.y_ps, 1)
                scatter(s, 1, steps + 1).then_inc(s.scattered, 1)
                pe.wait_ge(s.xe, steps + 1 + s.g)
                pe.wait_ge(s.gpt, steps + 2 + s.z)

            def moe(layer, u0):
                router(layer)
                pe.wait_ge(xs_sb, 2 * (layer + 1))
                pe.wait_ge(flag_sb, layer + 1)
                experts(fast[layer], slot_full, NE, u0)
                over = pe.value_load(flag[0:1, layer, 0:1])
                with pe.If(over > CAP):
                    experts(more[layer], more_full[layer], NIT - NE, 0)
                with pe.Else():
                    pe.nop()
                for b in (0, 2, 1, 3):
                    mm(psum[b][:], zeros_b[:], zeros_row, start=False, stop=True).then_inc(mix_ps, 1)

            def gdn():
                transpose_x(2)
                pe.wait_ge(gdn_in, 80)
                transpose(psum[7][:, 0:P], cw_in, ident).then_inc(cw_ps, 1)
                pe.wait_ge(xT_sb, 12)
                for j in range(DJ):
                    last = mm(psum[3][0:48, 0:SEQ], wba[:, j], xT[:, j], start=(j == 0), stop=(j == DJ - 1))
                last.then_inc(ba_ps, 1)

                def project(n):
                    if n >= 2:
                        pe.wait_ge(xc_sb, n - 1)
                    for i in range(2):
                        ch = 2 * n + i
                        u = UNIT_GDN + ch // 4
                        if ch % 4 == 0:
                            slot_ready(u)
                        for j in range(DJ):
                            last = mm(psum[n % 2][:, i * SEQ:(i + 1) * SEQ],
                                      ring[:, u % RING, j, (ch % 4) * P:(ch % 4 + 1) * P], xT[:, j],
                                      start=(j == 0), stop=(j == DJ - 1))
                    last.then_inc(cv_ps, 1)

                def squares(m):
                    pe.wait_ge(sq_sb, m + 1)
                    mm(psum[2][:], k("ones"), sq.rearrange("p a b -> p (a b)"), start=True, stop=True).then_inc(ss_ps, 1)

                def v_tokens(m):
                    h = m - 8
                    pe.wait_ge(si_sb, m + 1)
                    if h >= 2:
                        pe.wait_ge(vt_sb, h - 1)
                    for c in range(NC_):
                        last = transpose(psum[6 + m % 2][:, c * P:(c + 1) * P], vT[:, m % 2, c].rearrange("p e i -> p (e i)"), ident)
                    last.then_inc(vt_ps, 1)

                for n in range(18):
                    if n < 16:
                        project(n)
                    if 2 <= n < 10:
                        squares(n - 2)
                    if n >= 10:
                        v_tokens(n - 2)
                    if n == 4:
                        pe.wait_ge(gc_sb, 1)
                        for w in range(2):
                            src = gT[0:16, 2] if w else gcT[:]
                            for c in range(NC_):
                                for e in range(2):
                                    last = mm(psum[3][e * C:(e + 1) * C, (w * NC_ + c) * GH:(w * NC_ + c + 1) * GH],
                                              src[:, c * C:(c + 1) * C], ident[0:16, e:16:2], start=True, stop=True)
                        last.then_inc(col_ps, 1)
                pe.wait_ge(qk_sb, 8)
                pe.wait_ge(xc_sb, 16)
                pe.wait_ge(vt_sb, 8)
                pe.wait_ge(col_sb, 1)
                for half in range(2):
                    hs = range(4 * half, 4 * half + 4)
                    if half:
                        pe.wait_ge(oq_sb, 12)
                        pe.wait_ge(ao_sb, 16)
                    for h in hs:
                        n = h - 4 * half
                        bank = psum[n][:].rearrange("p (c e i) -> p c e i", c=NC_, e=2)
                        for e in range(2):
                            last = mm(bank[:, :, e], ident[0:16, 2 * h + e:2 * h + e + 1].to_broadcast([16, P]),
                                      gcT[:], start=True, stop=True)
                        last.then_inc(row_ps, 1)
                    for h in hs:
                        for g in range(2):
                            i = 2 * h + g
                            bank = psum[4 + i % 4]
                            if h - 4 * half >= 2:
                                pe.wait_ge(kk_sb, i - 3)
                            for cc in range(2):
                                c = 2 * g + cc
                                src = gq[:, :, h, c * C:(c + 1) * C].unsqueeze(2).to_broadcast([P, 2, 2, C])
                                for e in range(2):
                                    last = mm(bank[e * C:(e + 1) * C, cc * 2 * P:(cc + 1) * 2 * P],
                                              gq[:, 1, h, c * C:(c + 1) * C], src, start=True, stop=True)
                            last.then_inc(kk_ps, 1)
                    for lv in range(LEVELS):
                        for n in range(4):
                            g = (half * LEVELS + lv) * 4 + n
                            if lv == 0:
                                pe.wait_ge(kk_sb, 2 * (4 * half + n) + 2)
                                pe.wait_ge(tri_init, 4 * half + n + 1)
                            else:
                                pe.wait_ge(tt_sb, g - 3)
                            for c in range(NC_):
                                last = mm(psum[n][:, c * P:(c + 1) * P], nlt[:, n, c], tri[:, n, c], start=True, stop=True)
                            last.then_inc(ly_ps, 1)
                        for n in range(4):
                            g = (half * LEVELS + lv) * 4 + n
                            pe.wait_ge(ly_sb, g + 1)
                            for c in range(NC_):
                                last = mm(psum[4 + n][:, c * P:(c + 1) * P], triT[:, n, c], ty[:, n, c], start=True, stop=True)
                            last.then_inc(tl_ps, 1)
                        for n in range(4):
                            g = (half * LEVELS + lv) * 4 + n
                            pe.wait_ge(tri_sb, g + 1)
                            for c in range(NC_):
                                last = transpose(psum[n][:, c * P:(c + 1) * P], tri[:, n, c], ident)
                            last.then_inc(tt_ps, 1)
                    pe.wait_ge(tt_sb, (half + 1) * LEVELS * 4)
                    for n in range(4):
                        for c in range(NC_):
                            for e in range(2):
                                last = mm(psum[n][e * C:(e + 1) * C, c * P:(c + 1) * P],
                                          gq[:, 1, 4 * half + n, c * C:(c + 1) * C], ident, start=True, stop=True)
                        last.then_inc(kt_ps, 1)
                    pe.wait_ge(kt_sb, 4 * half + 4)

                    def read_state(g):
                        c, n = g // 4, g % 4
                        h = 4 * half + n
                        G = half * 16 + g
                        if c == 0:
                            return
                        pe.wait_ge(st_sb, half * 12 + 4 * (c - 1) + n + 1)
                        if g >= 6:
                            pe.wait_ge(r_sb, G - 1)
                            pe.wait_ge(oq_sb, half * 12 + g - 4 - 1)
                        bank = psum[g % 2]
                        for w in (1, 0):
                            for e in range(2):
                                last = mm(bank[e * C:(e + 1) * C, w * P:(w + 1) * P], gq[:, w, h, c * C:(c + 1) * C],
                                          state[:, 2 * n + e], start=True, stop=True)
                        last.then_inc(ks_ps, 1)

                    def solve(g):
                        c, n = g // 4, g % 4
                        G = half * 16 + g
                        if c:
                            pe.wait_ge(r_sb, G + 1)
                        if g >= 2:
                            pe.wait_ge(vd_sb, G - 1)
                            pe.wait_ge(vn_sb, G - 1)
                        rhs = rres[:, g % 2] if c else vtok[:, 0, 4 * half + n]
                        mm(psum[2 + g % 2][:, 0:P], triT[:, n, c], rhs, start=True, stop=True).then_inc(tr2_ps, 1)

                    def finish(g):
                        c, n = g // 4, g % 4
                        G = half * 16 + g
                        pe.wait_ge(vn_sb, G + 1)
                        if g >= 2:
                            pe.wait_ge(ao_sb, G - 1)
                        mm(psum[4 + g % 2][:, 0:P], att[:, n, c], vnew[:, g % 2], start=True, stop=True).then_inc(ao_ps, 1)
                        if c < NC_ - 1:
                            pe.wait_ge(vd_sb, G + 1)
                            if g >= 1:
                                pe.wait_ge(st_sb, half * 12 + g)
                            for e in range(2):
                                part = slice(e * C, (e + 1) * C)
                                last = mm(psum[6 + e][:, 0:P], ktok[part, c, n], vdec[part, g % 2], start=True, stop=True)
                            last.then_inc(su_ps, 1)

                    for g in range(18):
                        if g < 16:
                            read_state(g)
                        if 1 <= g <= 16:
                            solve(g - 1)
                        if g >= 2:
                            finish(g - 2)
                for zz in range(4):
                    u = UNIT_GDN + 8 + zz
                    slot_ready(u)
                    w = ring[:, u % RING].rearrange("p j (h e d) -> p j h e d", h=2, e=2)
                    for cp in range(2):
                        i = 2 * zz + cp
                        if i >= 2:
                            pe.wait_ge(og_sb, i - 1)
                        else:
                            pe.wait_ge(ao_sb, 32)
                        for cc in range(2):
                            c = 2 * cp + cc
                            for j in range(DJ):
                                for e in range(2):
                                    last = mm(psum[i % 2][e * C:(e + 1) * C, cc * SEQ:(cc + 1) * SEQ],
                                              xT[:, j, c * C:(c + 1) * C], w[:, j, :, e], start=(j == 0), stop=(j == DJ - 1))
                        last.then_inc(z_ps, 1)
                        if i >= 1:
                            gated_transpose(i - 1)
                gated_transpose(7)
                pe.wait_ge(gt_sb, 8)
                for u in range(UNIT_GDN + 12, UNIT_GDN + 16):
                    slot_ready(u)
                for t in range(NT):
                    for h in range(2):
                        for c in range(2 * GH):
                            u = UNIT_GDN + 12 + 2 * h + c // 8
                            last = mm(psum[2 * h + t][:], goT[:, c, t * P:(t + 1) * P], ring[:, u % RING, c % 8],
                                      start=(c == 0), stop=(c == 2 * GH - 1))
                        last.then_inc(mix_ps, 1)

            def gated_transpose(i):
                zz, cp = i // 2, i % 2
                pe.wait_ge(og_sb, i + 1)
                if i >= 2:
                    pe.wait_ge(gt_sb, i - 1)
                for hh in range(2):
                    for cc in range(2):
                        last = transpose(psum[2 + i % 2][:, (2 * hh + cc) * P:(2 * hh + cc + 1) * P],
                                         vtok[:, 2 * cp + cc, 2 * zz + hh], ident)
                last.then_inc(gt_ps, 1)

            attention()
            moe(0, UNIT_MOE0)
            gdn()
            moe(1, UNIT_MOE1)

        @block.scalar
        def _(act):
            do = nc.scalar.activation
            own = Own(act, own_act)

            def copy(o, i, **kw):
                return do(o, i, ACT.Copy, **kw)

            def inverse_root(n):
                for t in range(NT):
                    var, r = spread[:, t, 0:1], spread[:, t, 1:2]
                    act.wait_ge(var_sb, 2 * n + t + 1)
                    own.link(do(r, var, ACT.Ln))
                    do(r, r, ACT.Exp, scale=-0.5).then_inc(rstd_sb, 1)

            def evacuate_xT(n):
                for b in range(4):
                    act.wait_ge(xT_ps, 4 * n + b + 1)
                    copy(xT[:, 2 * b:2 * b + 2], psum[b][:].rearrange("p (j t) -> p j t", j=2)).then_inc(xT_sb, 1)

            def attention():
                evacuate_xT(0)

                def evacuate_qkT(i):
                    g, w = i // 2, i % 2
                    for t in range(NT):
                        act.wait_ge(tr_ps, 2 * i + t + 1)
                        copy(qkT[:, w, 4 * g:4 * g + 4, t * P:(t + 1) * P],
                             psum[6 + t][:].rearrange("p (q t) -> p q t", q=4)).then_inc(qkT_sb, 1)

                for g in range(2):
                    evacuate_qkT(2 * g)
                    for t in range(NT):
                        act.wait_ge(proj_ps, 6 * g + 4 + t + 1)
                        copy(vtk[:, t, g * HALF:(g + 1) * HALF], psum[4 + t][:]).then_inc(v_sb, 1)
                    evacuate_qkT(2 * g + 1)
                for n in range(HEADS + 3):
                    if n < HEADS:
                        act.wait_ge(max_sb, n + 1)
                        b = n % 4
                        do(s_sb[:, b, 0:P], s_sb[:, b, 0:P], ACT.Exp, bias=neg_max[:, b, 0:1], accum_out=row_sum[:, b, 0:1]
                           ).then_inc(exp_sb, 1)
                        do(s_sb[:, b, P:3 * P], s_sb[:, b, P:3 * P], ACT.Exp, bias=neg_max[:, b, 1:2],
                           accum_out=row_sum[:, b, 1:2]).then_inc(exp_sb, 1)
                    if 2 <= n < HEADS + 2:
                        act.wait_ge(pT_ps, n - 1)
                        if n >= 4:
                            act.wait_ge(o_ps, n - 3)
                        copy(pT[:, n % 2], psum[2 + n % 2][:, 0:384]).then_inc(pT_sb, 1)
                    if n >= 3 and n % 2 == 0:
                        pair = (n - 4) // 2
                        act.wait_ge(o_ps, 2 * pair + 2)
                        copy(oT[:, pair], psum[4 + pair % 2][:, 0:SEQ]).then_inc(oT_sb, 1)

            def moe(layer):
                evacuate_xT(1 + 2 * layer)
                for t in range(NT):
                    act.wait_ge(x_ready, 4 * layer + 1 + t)
                    copy(xs[:, t, 0], x[:, t].rearrange("p (q j) -> p j q", j=DJ)).then_inc(part_act, 1)
                act.wait_ge(lgT_ps, layer + 1)
                copy(lgT[0:NE], psum[4][0:NE, 0:SEQ]).then_inc(lgT_sb, 1)
                act.wait_ge(lg_ps, layer + 1)
                do(scores.rearrange("p t e -> p (t e)"), psum[5][:, 0:NT * NE], ACT.Exp, scale=-1.0).then_inc(sc_sb, 1)
                for t in range(NT):
                    act.wait_ge(left_sb, 2 * layer + t + 1)
                    copy(xs[:, t, 1], res[:, t].rearrange("p (j q) -> p j q", j=DJ)).then_inc(part_act, 1)

                def experts(s, steps):
                    act.wait_ge(s.gathered, 1 + s.g)
                    copy(xeT.rearrange("p j s -> p (j s)"), psum[4][:]).then_inc(s.xe, 1)
                    with act.Fori(0, steps) as n:
                        act.wait_ge(s.h_ps, n + (1 + s.e))
                        do(eh, psum[5][:, 0:SEQ], ACT.Tanh, scale=0.5).then_inc(s.sig, 1)
                        act.wait_ge(s.hT_ps, n + (1 + s.e))
                        copy(hT.rearrange("p c g s -> p (c g s)"), psum[6][:, 0:SEQ]).then_inc(s.hT, 1)
                        act.wait_ge(s.gathered, n + (2 + s.g))
                        copy(xeT.rearrange("p j s -> p (j s)"), psum[4][:]).then_inc(s.xe, 1)

                act.wait_ge(flag_sb, layer + 1)
                experts(fast[layer], NE)
                over = act.value_load(flag[0:1, layer, 0:1])
                with act.If(over > CAP):
                    experts(more[layer], NIT - NE)
                with act.Else():
                    act.nop()

            def gdn():
                evacuate_xT(2)
                act.wait_ge(cw_ps, 1)
                copy(cw[:], psum[7][:, 0:P]).then_inc(cw_sb, 1)
                act.wait_ge(ba_ps, 1)
                do(gT[0:16, 4], psum[3][0:16, 0:SEQ], ACT.Exp, scale=-1.0).then_inc(ba_exp, 1)
                do(ab[32:48, 2:3], ab[32:48, 1:2], ACT.Exp).then_inc(ba_exp, 1)
                act.wait_ge(ba_ab, 1)
                own.link(do(gT[32:48, 1], gT[32:48, 1], ACT.Exp))
                do(gT[32:48, 1], gT[32:48, 1], ACT.Ln, bias=1.0).then_inc(ba_sp, 1)

                for n in range(18):
                    if n < 16:
                        act.wait_ge(cv_ps, n + 1)
                        if n >= 2:
                            act.wait_ge(cv_sb, n - 1)
                        else:
                            act.wait_ge(init, 6)
                        copy(xc[:, n % 2, :, TAPS - 1:], psum[n % 2][:].rearrange("p (i t) -> p i t", i=2)
                             ).then_inc(xc_sb, 1)
                    if 1 <= n <= 16:
                        act.wait_ge(cv_sb, n)
                        if n >= 3:
                            act.wait_ge(si_sb, n - 2)
                        do(ce[:, (n - 1) % 2], cv[:, (n - 1) % 2], ACT.Exp, scale=-1.0).then_inc(ce_sb, 1)
                    if 2 <= n < 10:
                        m = n - 2
                        act.wait_ge(si_sb, m + 1)
                        do(sq, gq[:, m // 4, 2 * (m % 4):2 * (m % 4) + 2], ACT.Square).then_inc(sq_sb, 1)
                        act.wait_ge(ss_ps, m + 1)
                        if m:
                            act.wait_ge(qk_sb, m)
                        own.link(do(rn.rearrange("p a b -> p (a b)"), psum[2][:], ACT.Ln, bias=eps[:]))
                        do(rn, rn, ACT.Exp, scale=-0.5).then_inc(ss_sb, 1)
                    if n == 5:
                        act.wait_ge(col_sb, 1)
                        do(gcol[:, 2], gcol[:, 0], ACT.Exp).then_inc(col_exp, 1)
                    if n >= 10:
                        h = n - 10
                        act.wait_ge(vt_ps, h + 1)
                        copy(vtok[:, :, h], psum[6 + h % 2][:].rearrange("p (c d) -> p c d", c=NC_)).then_inc(vt_sb, 1)
                for half in range(2):
                    for n in range(4):
                        h = 4 * half + n
                        rowv = psum[n][:].rearrange("p (c e i) -> p c e i", c=NC_, e=2)
                        act.wait_ge(dm_sb, h + 1)
                        do(sdec[:, h], rowv[:, :, :, C - 1], ACT.Exp).then_inc(dt_sb, 1)
                        do(ty[:, n], ty[:, n], ACT.Exp).then_inc(dt_sb, 1)
                    dec = gcol[:, 5].rearrange("p (c h) -> p c h", h=GH)[:, :, 4 * half:4 * half + 4]
                    do(dec, dec, ACT.Exp).then_inc(dec_exp, 1)
                    for lv in range(LEVELS):
                        for n in range(4):
                            g = (half * LEVELS + lv) * 4 + n
                            act.wait_ge(ly_ps, g + 1)
                            if lv == 0:
                                act.wait_ge(kk_sb, 2 * (4 * half + n) + 2)
                            copy(ty[:, n].rearrange("p c i -> p (c i)"), psum[n][:]).then_inc(ly_sb, 1)
                        for n in range(4):
                            g = (half * LEVELS + lv) * 4 + n
                            act.wait_ge(tt_ps, g + 1)
                            copy(triT[:, n].rearrange("p c i -> p (c i)"), psum[n][:]).then_inc(tt_sb, 1)
                    for n in range(4):
                        act.wait_ge(kt_ps, 4 * half + n + 1)
                        copy(ktok[:, :, n], psum[n][:].rearrange("p (c d) -> p c d", c=NC_)).then_inc(kt_sb, 1)
                    for g in range(17):
                        G = half * 16 + g
                        c, n = g // 4, g % 4
                        u = c * GH + 4 * half + n
                        if g >= 1:
                            g1 = g - 1
                            G1 = G - 1
                            c, n = g1 // 4, g1 % 4
                            u = c * GH + 4 * half + n
                            act.wait_ge(tr2_ps, G1 + 1)
                            if g1 >= 2:
                                act.wait_ge(ao_ps, G1 - 1)
                                act.wait_ge(vd_sb, G1 - 1)
                            copy(vnew[:, g1 % 2], psum[2 + g1 % 2][:, 0:P], scale=gcol[:, 1, u:u + 1]).then_inc(vn_sb, 1)
                        if g < 16 and g >= 4:
                            u = g // 4 * GH + 4 * half + g % 4
                            act.wait_ge(r_sb, G + 1)
                            if g >= 6:
                                act.wait_ge(ao_sb, G - 1)
                            copy(oq[:, g % 2], psum[g % 2][:, 0:P], scale=gcol[:, 3, u:u + 1]).then_inc(oq_sb, 1)
                act.wait_ge(ao_sb, 32)
                for u in range(32):
                    c, h = u // GH, u % GH
                    if u:
                        own.wait()
                    own(do(zt[:, 0, 0:P], vtok[:, c, h], ACT.Square, accum_out=gcol[:, 7, u:u + 1]))
                own.wait()
                own.link(do(gcol[:, 7], gcol[:, 7], ACT.Ln, bias=eps[:], scale=1.0 / GD))
                do(gcol[:, 7], gcol[:, 7], ACT.Exp, scale=-0.5).then_inc(rms_sb, 1)
                for i in range(9):
                    if i < 8:
                        act.wait_ge(z_ps, i + 1)
                        if i >= 2:
                            act.wait_ge(og_sb, i - 1)
                        else:
                            own.wait()
                        do(zt[:, i % 2], psum[i % 2][:], ACT.Exp, scale=-1.0).then_inc(z_exp, 1)
                    if i >= 1:
                        m = i - 1
                        zz, cp = m // 2, m % 2
                        act.wait_ge(gt_ps, m + 1)
                        for hh in range(2):
                            dst = goT[:, 2 * (2 * zz + hh):2 * (2 * zz + hh) + 2, 2 * cp * C:2 * (cp + 1) * C]
                            ins = copy(dst.rearrange("p e (c i) -> p c e i", c=2),
                                       psum[2 + m % 2][:, 2 * hh * P:2 * (hh + 1) * P].rearrange(
                                           "p (c e i) -> p c e i", c=2, e=2))
                            if hh:
                                ins.then_inc(gt_sb, 1)
                            else:
                                own(ins)

            attention()
            inverse_root(0)
            moe(0)
            inverse_root(1)
            gdn()
            inverse_root(2)
            moe(1)
            inverse_root(3)

        @block.vector
        def _(dve):
            v = nc.vector
            own = Own(dve, own_dve)

            def layer_norm(n):
                for t in range(NT):
                    for h in range(2):
                        dve.wait_ge(mix_ps, 4 * n + 2 * t + h + 1)
                        col = slice(h * HALF, (h + 1) * HALF)
                        ins = v.scalar_tensor_tensor(out=y[:, t, col], in0=x[:, t, col], scalar=ALPHA,
                                                     in1=psum[2 * h + t][:], op0=ALU.mult, op1=ALU.add)
                        if h:
                            ins.then_inc(y_sb, 1)
                            dve.wait_ge(y_sb, 2 * n + t + 1)
                        else:
                            own.link(ins)
                        own(v.bn_stats(stats[:, t, h], y[:, t, col]))
                    own.wait()
                    own.link(v.bn_aggr(mv[:, t], stats[:, t]))
                    v.tensor_scalar(out=spread[:, t, 0:1], in0=mv[:, t, 1:2], scalar1=LN_EPS, scalar2=None,
                                    op0=ALU.add).then_inc(var_sb, 1)
                dve.wait_ge(ln_in, 32 * (n + 1))
                for t in range(NT):
                    own(v.scalar_tensor_tensor(out=y[:, t], in0=y[:, t], scalar=mv[:, t, 0:1], in1=lnp[:, 0],
                                               op0=ALU.subtract, op1=ALU.mult))
                for t in range(NT):
                    var, r, w = (spread[:, t, i:i + 1] for i in range(3))
                    dve.wait_ge(rstd_sb, 2 * n + t + 1)
                    own.link(v.tensor_tensor(out=w, in0=r, in1=r, op=ALU.mult))
                    own.link(v.tensor_tensor(out=w, in0=w, in1=var, op=ALU.mult))
                    own.link(v.tensor_scalar(out=w, in0=w, scalar1=-0.5, scalar2=1.5, op0=ALU.mult, op1=ALU.add))
                    own.link(v.tensor_tensor(out=r, in0=r, in1=w, op=ALU.mult))
                    v.scalar_tensor_tensor(out=x[:, t], in0=y[:, t], scalar=r, in1=lnp[:, 1], op0=ALU.mult,
                                           op1=ALU.add).then_inc(x_ready, 1)

            def attention():
                dve.wait_ge(const_in, 16)
                cos = k("cos").rearrange("p (t a h d) -> p t a h d", t=NT, a=1, h=1)
                sin = k("sin").rearrange("p (t a h d) -> p t a h d", t=NT, a=1, h=1)
                i = 0
                for n in range(6):
                    if n % 3 == 2:
                        continue
                    for t in range(NT):
                        dve.wait_ge(proj_ps, 2 * n + t + 1)
                        if i >= 2:
                            dve.wait_ge(tr_ps, i - 1)
                        src = psum[4 + t][:].rearrange("p (a d) -> p a d", d=32)
                        o4 = qk_tok[:, t].rearrange("p (a h d) -> p a h d", h=2, d=32)
                        o3 = qk_tok[:, t].rearrange("p (a d) -> p a d", d=32)
                        r4 = rot[:, t].rearrange("p (a h d) -> p a h d", h=2, d=32)
                        r3 = rot[:, t].rearrange("p (a d) -> p a d", d=32)
                        cb = cos[:, t, 0].to_broadcast([P, 16, 32])
                        sb_ = sin[:, t, 0].to_broadcast([P, 16, 32])
                        own(v.tensor_tensor(out=o3, in0=src, in1=cb, op=ALU.mult))
                        own.link(v.tensor_tensor(out=r3, in0=src, in1=sb_, op=ALU.mult))
                        own(v.tensor_tensor(out=o4[:, :, 0], in0=o4[:, :, 0], in1=r4[:, :, 1], op=ALU.subtract))
                        own.link(v.tensor_tensor(out=o4[:, :, 1], in0=o4[:, :, 1], in1=r4[:, :, 0], op=ALU.add))
                        dve.sem_inc(rope_sb, 1)
                        i += 1
                dve.wait_ge(small_in, 64)
                own(v.tensor_copy(upper_b[:], k("upper")))
                own(v.tensor_copy(ones_b[:], k("ones")))
                own(v.tensor_copy(levels[:], levels_in))
                for n in range(HEADS + 1):
                    if n < HEADS:
                        b = n % 4
                        dve.wait_ge(s_ps, n + 1)
                        if n >= 4:
                            dve.wait_ge(pT_ps, n - 3)
                        v.scalar_tensor_tensor(out=s_sb[:, b], in0=psum[n % 2][:, 0:384], scalar=ATT_SCALE,
                                               in1=k("mask_a" if n < 8 else "mask_b"), op0=ALU.mult,
                                               op1=ALU.add).then_inc(s_read, 1)
                        dve.wait_ge(s_read, n + 1)
                        own(v.tensor_reduce(out=neg_max[:, b, 0:1], in_=s_sb[:, b, 0:P], axis=AX, op=ALU.max))
                        own.link(v.tensor_reduce(out=neg_max[:, b, 1:2], in_=s_sb[:, b, P:384], axis=AX, op=ALU.max))
                        v.tensor_scalar(out=neg_max[:, b], in0=neg_max[:, b], scalar1=-1.0, scalar2=None,
                                        op0=ALU.mult).then_inc(max_sb, 1)
                    if n >= 1:
                        m = n - 1
                        b = m % 4
                        dve.wait_ge(exp_sb, 2 * m + 2)
                        own.link(v.reciprocal(row_sum[:, b], row_sum[:, b]))
                        own(v.tensor_scalar(out=s_sb[:, b, 0:P], in0=s_sb[:, b, 0:P], scalar1=row_sum[:, b, 0:1],
                                            scalar2=None, op0=ALU.mult))
                        own.link(v.tensor_scalar(out=s_sb[:, b, P:384], in0=s_sb[:, b, P:384], scalar1=row_sum[:, b, 1:2],
                                                 scalar2=None, op0=ALU.mult))
                        dve.sem_inc(p_sb, 1)
                layer_norm(0)

            def route(layer):
                iota = k("iota")

                def over(view, n, at):
                    view = view.unsqueeze(at)
                    shape = list(view.shape)
                    shape[at] = n
                    return view.to_broadcast(shape)

                own(v.memset(gsum, NEG))
                own(v.memset(gate, 0.0))
                own(v.memset(pos, -1.0))
                dve.wait_ge(sc_sb, layer + 1)
                own.link(v.tensor_scalar(out=scores, in0=scores, scalar1=1.0, scalar2=None, op0=ALU.add))
                own.link(v.reciprocal(scores, scores))
                own.link(v.tensor_tensor(out=sel, in0=scores, in1=over(rbias[:], NT, 1), op=ALU.add))
                for t in range(NT):
                    for g in range(NG):
                        own(v.max(out=top[:, t, g], in_=sel[:, t, g * EG:(g + 1) * EG]))
                own.wait()
                own.link(v.tensor_tensor(out=gsum[:, :, 0:NG], in0=top[:, :, :, 0], in1=top[:, :, :, 1], op=ALU.add))
                for t in range(NT):
                    own(v.max(out=m8[:, t], in_=gsum[:, t]))
                own.wait()
                for t in range(NT):
                    own(v.max_index(out=i8[:, t], in_max=m8[:, t], in_values=gsum[:, t]))
                own.wait()
                own.link(v.tensor_tensor(out=goh, in0=over(iota[:, 0:NG], NT, 1),
                                         in1=i8[:, :, 0:1].to_broadcast([P, NT, NG]), op=ALU.is_equal))
                by_group = t32.rearrange("p t (e g) -> p t e g", g=NG)
                own.link(v.tensor_tensor(out=by_group, in0=sel.rearrange("p t (g e) -> p t e g", g=NG),
                                         in1=over(goh, EG, 2), op=ALU.mult))
                own.link(v.tensor_reduce(out=ing, in_=by_group, axis=AX, op=ALU.add))
                for t in range(NT):
                    own(v.max(out=m8[:, t], in_=ing[:, t]))
                own.wait()
                for t in range(NT):
                    own(v.max_index(out=i8[:, t], in_max=m8[:, t], in_values=ing[:, t]))
                own.wait()
                own.link(v.tensor_tensor(out=loh, in0=over(over(iota[:, 0:EG], 2, 1), NT, 1),
                                         in1=i8[:, :, 0:2].unsqueeze(3).to_broadcast([P, NT, 2, EG]), op=ALU.is_equal))
                own.link(v.tensor_tensor(out=pair, in0=loh[:, :, 0], in1=loh[:, :, 1], op=ALU.add))
                own.link(v.tensor_tensor(out=both.rearrange("p t (g e) -> p t g e", g=NG), in0=over(goh, EG, 3),
                                         in1=over(pair, NG, 2), op=ALU.mult))
                v.tensor_copy(both_b, both).then_inc(a_sb, 1)
                own.link(v.tensor_tensor(out=t32, in0=both, in1=scores, op=ALU.mult))
                own.link(v.tensor_reduce(out=gs, in_=t32, axis=AX, op=ALU.add))
                own.link(v.reciprocal(gs, gs))
                for t in range(NT):
                    own(v.tensor_scalar(out=gate[:, t, 0:NIT].rearrange("p (q e) -> p q e", e=NE),
                                        in0=over(t32[:, t], PASSES, 1), scalar1=gs[:, t:t + 1], scalar2=None,
                                        op0=ALU.mult))
                own.wait()
                dve.wait_ge(rank_ps, layer + 1)
                own(v.tensor_reduce(out=cnt, in_=psum[6][:, 2 * NE:3 * NE], axis=AX, op=ALU.max))
                own.link(v.scalar_tensor_tensor(out=t32, in0=psum[6][:, 0:2 * NE].rearrange("p (t e) -> p t e", t=NT),
                                                scalar=1.0, in1=both, op0=ALU.add, op1=ALU.mult))
                for q in range(PASSES):
                    own(v.tensor_scalar(out=pos[:, :, q * NE:(q + 1) * NE], in0=t32, scalar1=-1.0 - q * CAP,
                                        scalar2=None, op0=ALU.add))
                dve.wait_ge(init, 2)
                v.tensor_copy(flag[:, layer, 0:1], cnt).then_inc(flag_sb, 1)
                own.wait()

            def experts(s, steps, base):
                o2 = Own(dve, s.own)
                o2.n = s.o

                def picks(n, b):
                    for t in range(NT):
                        at = pos[:, t, bass.ds(n + base, 1)]
                        o2(v.tensor_scalar(out=pick[:, b, t], in0=k("iota"), scalar1=at, scalar2=None, op0=ALU.is_equal))
                        ins = v.tensor_scalar(out=gpick[:, b, t], in0=k("iota").unsqueeze(1).to_broadcast([P, 2, CAP]),
                                              scalar1=at, scalar2=gate[:, t, bass.ds(n + base, 1)],
                                              op0=ALU.is_equal, op1=ALU.mult)
                        o2(ins)
                    o2.wait()
                    dve.sem_inc(s.pick, 1)

                o2(v.memset(y_e, 0.0))
                o2.link(v.memset(gpT[:, 1], 0.0))
                dve.sem_inc(s.y, 1)
                dve.sem_inc(s.gpt, 1)
                picks(0, 0)
                dve.wait_ge(s.gathered, 1 + s.g)
                o2.link(v.tensor_copy(gpT[:, 0].rearrange("p t q -> p (t q)"), psum[5][:, 0:SEQ]))
                dve.sem_inc(s.gpt, 1)
                n0, per = o2.n, OWN_STEP
                assert n0 == s.o + OWN_HEAD
                with dve.Fori(0, steps // 2) as i:
                    for b in range(2):
                        n = i * 2 + b
                        o2.n, o2.loop = n0 + per * b, i * (2 * per)
                        picks(n + 1, 1 - b)
                        dve.wait_ge(s.sig, n + (1 + s.e))
                        o2.link(v.scalar_tensor_tensor(out=hg, in0=eh, scalar=1.0, in1=psum[5][:, 0:SEQ], op0=ALU.add,
                                                       op1=ALU.mult))
                        v.scalar_tensor_tensor(out=hm.rearrange("p c q -> p q c"),
                                               in0=hg.rearrange("p (q c) -> p q c", c=2), scalar=0.5,
                                               in1=psum[5][:, SEQ:2 * SEQ].rearrange("p (q c) -> p q c", c=2),
                                               op0=ALU.mult, op1=ALU.mult).then_inc(s.hm, 1)
                        dve.wait_ge(s.gathered, n + (2 + s.g))
                        o2.link(v.tensor_copy(gpT[:, 1 - b].rearrange("p t q -> p (t q)"), psum[5][:, 0:SEQ]))
                        dve.sem_inc(s.gpt, 1)
                        dve.wait_ge(s.y_ps, n + (1 + s.e))
                        o2.link(v.tensor_copy(y_e, psum[7][:]))
                        dve.sem_inc(s.y, 1)
                        assert o2.n == n0 + per * (b + 1)

            def moe(layer):
                route(layer)
                experts(fast[layer], NE, 0)
                dve.wait_ge(flag_sb, layer + 1)
                over = dve.value_load(flag[0:1, layer, 0:1])
                with dve.If(over > CAP):
                    dve.wait_ge(fast[layer].scattered, 1 + fast[layer].runs)
                    experts(more[layer], NIT - NE, NE)
                with dve.Else():
                    dve.nop()
                layer_norm(1 + 2 * layer)

            def gdn():
                dve.wait_ge(ba_ps, 1)
                dve.wait_ge(gdn_in, 80)
                hi = slice(32, 48)
                own.link(v.tensor_scalar(out=gT[hi, 0], in0=psum[3][hi, 0:SEQ], scalar1=ab[hi, 0:1], scalar2=None,
                                         op0=ALU.add))
                own.link(v.tensor_scalar(out=gT[hi, 1], in0=gT[hi, 0], scalar1=-1.0, scalar2=None, op0=ALU.mult))
                v.tensor_tensor(out=gT[hi, 1], in0=gT[hi, 0], in1=gT[hi, 1], op=ALU.min).then_inc(ba_ab, 1)
                dve.wait_ge(ba_exp, 2)
                own(v.tensor_scalar(out=ab[hi, 3:4], in0=ab[hi, 2:3], scalar1=-1.0, scalar2=None, op0=ALU.mult))
                own.link(v.tensor_scalar(out=gT[0:16, 2], in0=gT[0:16, 4], scalar1=1.0, scalar2=None, op0=ALU.add))
                own(v.reciprocal(gT[0:16, 2], gT[0:16, 2]))
                dve.wait_ge(ba_sp, 1)
                own.link(v.scalar_tensor_tensor(out=gT[hi, 0], in0=gT[hi, 0], scalar=0.0, in1=gT[hi, 1], op0=ALU.max,
                                                op1=ALU.add))
                own.link(v.tensor_scalar(out=gT[0:16, 3], in0=gT[hi, 0], scalar1=ab[hi, 3:4], scalar2=None, op0=ALU.mult))
                for c in range(NC_):
                    col = slice(c * C, (c + 1) * C)
                    own(v.tensor_tensor_scan(out=gcT[:, col], data0=k("ones")[0:16, 0:C], data1=gT[0:16, 3, col],
                                             initial=0.0, op0=ALU.mult, op1=ALU.add))
                own.wait()
                dve.sem_inc(gc_sb, 1)
                dve.wait_ge(cw_sb, 1)
                for n in range(18):
                    if n < 16:
                        b = n % 2
                        dve.wait_ge(xc_sb, n + 1)
                        if n >= 2:
                            dve.wait_ge(si_sb, n - 1)
                        for tap in range(TAPS):
                            for i in range(2):
                                ch = 2 * n + i
                                wt = cw[:, tap * 32 + ch:tap * 32 + ch + 1]
                                src = xc[:, b, i, tap:tap + SEQ]
                                if tap == 0:
                                    own(v.tensor_scalar(out=cv[:, b, i], in0=src, scalar1=wt, scalar2=None, op0=ALU.mult))
                                else:
                                    own(v.scalar_tensor_tensor(out=cv[:, b, i], in0=src, scalar=wt, in1=cv[:, b, i],
                                                               op0=ALU.mult, op1=ALU.add))
                            own.wait()
                        dve.sem_inc(cv_sb, 1)
                    if 1 <= n <= 16:
                        m = n - 1
                        b = m % 2
                        dve.wait_ge(ce_sb, m + 1)
                        own.link(v.tensor_scalar(out=ce[:, b], in0=ce[:, b], scalar1=1.0, scalar2=None, op0=ALU.add))
                        own.link(v.reciprocal(ce[:, b], ce[:, b]))
                        if m < 8:
                            dst = gq[:, m // 4, 2 * (m % 4):2 * (m % 4) + 2]
                        else:
                            dst = vT[:, b].rearrange("p c e i -> p e c i")
                            if m >= 10:
                                dve.wait_ge(vt_ps, m - 9)
                        in0, in1 = cv[:, b], ce[:, b]
                        if m >= 8:
                            in0, in1 = (w.rearrange("p e (c i) -> p e c i", c=NC_) for w in (in0, in1))
                        v.tensor_tensor(out=dst, in0=in0, in1=in1, op=ALU.mult).then_inc(si_sb, 1)
                    if 2 <= n < 10:
                        m = n - 2
                        dve.wait_ge(ss_sb, m + 1)
                        dst = gq[:, m // 4, 2 * (m % 4):2 * (m % 4) + 2]
                        v.tensor_tensor(out=dst, in0=dst, in1=rn, op=ALU.mult).then_inc(qk_sb, 1)
                    if n == 4:
                        dve.wait_ge(col_ps, 1)
                        own.link(v.tensor_copy(gcol[:, 0:2].rearrange("p w u -> p (w u)"), psum[3][:, 0:64]))
                        dve.sem_inc(col_sb, 1)
                    if n == 6:
                        dve.wait_ge(col_exp, 1)
                        own(v.tensor_scalar(out=gcol[:, 3], in0=gcol[:, 2], scalar1=GDN_SCALE, scalar2=None, op0=ALU.mult))
                        own(v.tensor_scalar(out=gcol[:, 4], in0=gcol[:, 2], scalar1=-1.0, scalar2=None, op0=ALU.mult))
                        own(v.tensor_scalar(out=gcol[:, 6], in0=gcol[:, 1], scalar1=-1.0, scalar2=None, op0=ALU.mult))
                        own.wait()
                for half in range(2):
                    for n in range(4):
                        h = 4 * half + n
                        dve.wait_ge(row_ps, h + 1)
                        if half:
                            dve.wait_ge(ao_sb, 16)
                            dve.wait_ge(tt_ps, LEVELS * 4)
                        for c in range(NC_):
                            u = c * GH + h
                            ins = v.scalar_tensor_tensor(out=ty[:, n, c], in0=psum[n][:, c * P:(c + 1) * P],
                                                         scalar=gcol[:, 0, u:u + 1], in1=k("decay_mask"),
                                                         op0=ALU.subtract, op1=ALU.add)
                            own(ins)
                        own.wait()
                        rowv = psum[n][:].rearrange("p (c e i) -> p c e i", c=NC_, e=2)
                        for e in range(2):
                            part = slice(e * C, (e + 1) * C)
                            own(v.tensor_tensor(out=gcol[part, 5].rearrange("p (c h) -> p c h", h=GH)[:, :, h],
                                                in0=rowv[part, :, e, C - 1],
                                                in1=gcol[part, 0].rearrange("p (c h) -> p c h", h=GH)[:, :, h],
                                                op=ALU.subtract))
                        own.wait()
                        dve.sem_inc(dm_sb, 1)
                    for n in range(4):
                        h = 4 * half + n
                        dve.wait_ge(dt_sb, 2 * h + 2)
                        for g in range(2):
                            dve.wait_ge(kk_ps, 2 * h + g + 1)
                            bank = psum[4 + (2 * h + g) % 4]
                            for cc in range(2):
                                c = 2 * g + cc
                                u = c * GH + h
                                own(v.scalar_tensor_tensor(out=att[:, n, c], in0=ty[:, n, c], scalar=GDN_SCALE,
                                                           in1=bank[:, cc * 2 * P:(cc * 2 + 1) * P], op0=ALU.mult,
                                                           op1=ALU.mult))
                                own(v.scalar_tensor_tensor(out=nlt[:, n, c], in0=ty[:, n, c],
                                                           scalar=gcol[:, 6, u:u + 1],
                                                           in1=bank[:, (cc * 2 + 1) * P:(cc * 2 + 2) * P], op0=ALU.mult,
                                                           op1=ALU.mult))
                            own.wait()
                            dve.sem_inc(kk_sb, 1)
                        for dst in (tri, triT):
                            own(v.tensor_copy(dst[:, n], ident.unsqueeze(1).to_broadcast([P, NC_, P])))
                        own.wait()
                        dve.sem_inc(tri_init, 1)
                    for lv in range(LEVELS):
                        for n in range(4):
                            g = (half * LEVELS + lv) * 4 + n
                            dve.wait_ge(tl_ps, g + 1)
                            v.copy_predicated(tri[:, n], levels[:, lv].unsqueeze(1).to_broadcast([P, NC_, P]),
                                              psum[4 + n][:].rearrange("p (c i) -> p c i", c=NC_)).then_inc(tri_sb, 1)
                    dve.wait_ge(dec_exp, half + 1)
                    own.link(v.memset(state, 0.0))
                    for g in range(18):
                        if g < 16 and g // 4:
                            c, n = g // 4, g % 4
                            u = c * GH + 4 * half + n
                            dve.wait_ge(ks_ps, half * 12 + g - 4 + 1)
                            if g >= 2:
                                dve.wait_ge(tr2_ps, half * 16 + g - 1)
                            v.scalar_tensor_tensor(out=rres[:, g % 2], in0=psum[g % 2][:, P:2 * P],
                                                   scalar=gcol[:, 4, u:u + 1], in1=vtok[:, c, 4 * half + n],
                                                   op0=ALU.mult, op1=ALU.add).then_inc(r_sb, 1)
                        elif g < 16:
                            dve.sem_inc(r_sb, 1)
                        if 1 <= g <= 16:
                            g1 = g - 1
                            c, n = g1 // 4, g1 % 4
                            u = c * GH + 4 * half + n
                            dve.wait_ge(vn_sb, half * 16 + g1 + 1)
                            if c < NC_ - 1:
                                if g1 >= 2:
                                    dve.wait_ge(su_ps, half * 12 + g1 - 1)
                                v.tensor_scalar(out=vdec[:, g1 % 2], in0=vnew[:, g1 % 2],
                                                scalar1=gcol[:, 5, u:u + 1], scalar2=None, op0=ALU.mult).then_inc(vd_sb, 1)
                            else:
                                dve.sem_inc(vd_sb, 1)
                        if g >= 2:
                            g2 = g - 2
                            G2 = half * 16 + g2
                            c, n = g2 // 4, g2 % 4
                            dve.wait_ge(ao_ps, G2 + 1)
                            dst = vtok[:, c, 4 * half + n]
                            if c:
                                dve.wait_ge(oq_sb, half * 12 + g2 - 4 + 1)
                                v.tensor_tensor(out=dst, in0=psum[4 + g2 % 2][:, 0:P], in1=oq[:, g2 % 2],
                                                op=ALU.add).then_inc(ao_sb, 1)
                            else:
                                v.tensor_copy(dst, psum[4 + g2 % 2][:, 0:P]).then_inc(ao_sb, 1)
                            if c < NC_ - 1:
                                dve.wait_ge(su_ps, half * 12 + g2 + 1)
                                for e in range(2):
                                    own(v.scalar_tensor_tensor(out=state[:, 2 * n + e], in0=state[:, 2 * n + e],
                                                               scalar=sdec[:, 4 * half + n, c, e:e + 1],
                                                               in1=psum[6 + e][:, 0:P], op0=ALU.mult, op1=ALU.add))
                                own.wait()
                                dve.sem_inc(st_sb, 1)
                dve.wait_ge(rms_sb, 1)
                for i in range(8):
                    zz, cp = i // 2, i % 2
                    z = zt[:, i % 2]
                    dve.wait_ge(z_exp, i + 1)
                    for cc in range(2):
                        for hh in range(2):
                            c, h = 2 * cp + cc, 2 * zz + hh
                            u = c * GH + h
                            own(v.scalar_tensor_tensor(out=vtok[:, c, h], in0=vtok[:, c, h], scalar=gcol[:, 7, u:u + 1],
                                                       in1=norm_g[:], op0=ALU.mult, op1=ALU.mult))
                    own.link(v.tensor_scalar(out=z, in0=z, scalar1=1.0, scalar2=None, op0=ALU.add))
                    own.link(v.reciprocal(z, z))
                    own.link(v.tensor_tensor(out=z, in0=psum[i % 2][:], in1=z, op=ALU.mult))
                    ot = vtok[:, 2 * cp:2 * cp + 2, 2 * zz:2 * zz + 2]
                    v.tensor_tensor(out=ot, in0=ot, in1=z.rearrange("p (c h d) -> p c h d", c=2, h=2),
                                    op=ALU.mult).then_inc(og_sb, 1)
                layer_norm(2)

            attention()
            moe(0)
            gdn()
            moe(1)


_INPUTS = ("x", "ab_w_in", "ab_w_out", "gdn_w_in", "gdn_conv_w", "gdn_a_log", "gdn_dt_bias", "gdn_norm_g", "gdn_w_out",
           "mix_ln_g", "mix_ln_b", "router_w", "router_bias", "moe_w1", "moe_w3", "moe_w2", "ffn_ln_g", "ffn_ln_b")


def kernel(**inputs):
    import concourse.bacc as bacc
    from concourse.bass_utils import run_bass_kernel_spmd

    nc = bacc.Bacc("TRN2", target_bir_lowering=False, num_devices=1)
    const, levels = tables()
    arrays = {name: np.ascontiguousarray(inputs[name]) for name in _INPUTS}
    arrays["const"], arrays["levels"] = const, levels
    aps = {name: nc.dram_tensor(f"in_{name}", v.shape, mybir.dt.from_np(v.dtype), kind="ExternalInput").ap()
           for name, v in arrays.items()}
    out = nc.dram_tensor("out", (1, SEQ, D), F32, kind="ExternalOutput").ap()
    build(nc, aps, out)
    r = run_bass_kernel_spmd(nc, [{f"in_{name}": v for name, v in arrays.items()}], core_ids=[0])
    return r.results[0]["out"]
```

```python
from contextlib import ExitStack

import numpy as np

import concourse.bass as bass
from concourse import mybir

F32 = mybir.dt.float32
BF16 = mybir.dt.bfloat16
I32 = mybir.dt.int32
U32 = mybir.dt.uint32
U8 = mybir.dt.uint8
ALU = mybir.AluOpType
ACT = mybir.ActivationFunctionType
AX = mybir.AxisListType.X

P = 128
D = 1024
SEQ = 256
NT = SEQ // P
DJ = D // P
HALF = 512
ALPHA = (2.0 * 2) ** 0.25
LN_EPS = 1e-5
NEG = -1e30

DH = 64
HEADS = 16
PAIRS = HEADS // 2
ATT_SCALE = DH ** -0.5

GH = 8
C = 64
NC_ = SEQ // C
GD = 128
GDN_SCALE = GD ** -0.5
NORM_EPS = 1e-6
TAPS = 4
QKV_CH = 4096
Z_BANKS = (0, 1, 4, 5)
ROW_BANKS = (2, 4)
LEVELS = 6

NE = 32
NG = 4
EG = NE // NG
CAP = 64
PASSES = SEQ // CAP
NIT = PASSES * NE

OWN_HEAD, OWN_STEP, OWN_LAST = 7, 7, 2

RING = 6
UNIT_ATT = 0
UNIT_MOE0 = UNIT_ATT + 8
UNIT_GDN = UNIT_MOE0 + 3 * NE
UNIT_MOE1 = UNIT_GDN + 16

COLS = {}
_at = 0
for _n, _w in (("ident", P), ("ones", P), ("upper", P), ("mask_a", 384), ("mask_b", 384), ("cos", 64), ("sin", 64),
               ("iota", CAP), ("decay_mask", P), ("alpha", P)):
    COLS[_n] = (_at, _w)
    _at += _w
N_CONST = _at


def tables():
    out = np.zeros((P, N_CONST), np.float32)
    p = np.arange(P)[:, None]

    def put(name, value):
        a, w = COLS[name]
        out[:, a:a + w] = value

    put("ident", p == np.arange(P)[None])
    put("alpha", ALPHA * (p == np.arange(P)[None]))
    put("ones", 1.0)
    put("upper", p < np.arange(P)[None])
    dist = np.concatenate([p - np.arange(P)[None], p + P - np.arange(SEQ)[None]], 1)
    put("mask_a", np.where(dist >= 0, 0.0, NEG))
    many = (dist <= 128).astype(int) + (dist % 4 == 0) + (dist % 16 == 0)
    put("mask_b", np.where((dist >= 0) & (many > 0), np.log(np.maximum(many, 1)), NEG))
    inv = 10000.0 ** (-np.arange(0, DH, 2, dtype=np.float32) / np.float32(DH))
    angle = np.arange(SEQ, dtype=np.float32)[:, None] * inv.astype(np.float32)[None]
    angle = angle.reshape(NT, P, DH // 2).transpose(1, 0, 2).reshape(P, NT * DH // 2)
    put("cos", np.cos(angle))
    put("sin", np.sin(angle))
    put("iota", np.arange(CAP)[None])
    q = np.arange(P)[None]
    put("decay_mask", np.where((p // C == q // C) & (p % C <= q % C), 0.0, NEG))
    levels = np.zeros((P, LEVELS, P), np.float32)
    for n in range(LEVELS):
        s = 1 << n
        i, j = (q, p) if n in (0, LEVELS - 1) else (p, q)
        levels[:, n] = (i // (2 * s) == j // (2 * s)) & (i % (2 * s) >= s) & (j % (2 * s) < s)
    return out, levels.reshape(P, LEVELS * P)


class Own:

    def __init__(self, eng, sem):
        self.eng, self.sem, self.n, self.loop = eng, sem, 0, None

    def __call__(self, ins):
        ins.then_inc(self.sem, 1)
        self.n += 1

    def wait(self):
        self.eng.wait_ge(self.sem, self.n if self.loop is None else self.loop + self.n)

    def link(self, ins):
        self(ins)
        self.wait()


def build(nc, a, out):
    with ExitStack() as ctx:
        def sb(name, shape, dt=F32):
            return ctx.enter_context(nc.sbuf_tensor(name, shape, dt))

        def sem(name):
            return ctx.enter_context(nc.semaphore(name))

        ring = sb("ring", [P, RING, DJ, HALF])
        x = sb("x", [P, NT, D])
        xT = sb("xT", [P, DJ, SEQ])
        y = sb("y", [P, NT, D])
        arena = sb("arena", [P, 72 * 256])
        const = sb("const", [P, N_CONST])
        levels = sb("levels", [P, LEVELS, P], U8)
        upper_b = sb("upper_b", [P, P], BF16)
        ones_b = sb("ones_b", [P, P], BF16)
        zeros_b = sb("zeros_b", [P, P], BF16)
        rw = sb("rw", [P, DJ, NE])
        rbias = sb("rbias", [P, NE])
        stats = sb("stats", [P, NT, 2, 6])
        mv = sb("mv", [P, NT, 2])
        spread = sb("spread", [P, NT, 3])
        eps = sb("eps", [P, 1])
        psum = [ctx.enter_context(nc.psum_tensor(f"bank{i}", [P, HALF], F32)) for i in range(8)]

        def k(name):
            at, w = COLS[name]
            return const[:, at:at + w]

        ident = k("ident")

        def area(kb, shape, dt=F32, size=4):
            n = int(np.prod(shape)) * size // 4
            at = int(kb * 256)
            v = arena[:, at:at + n]
            if dt != F32:
                v = v.bitcast(dt)
            if len(shape) == 1:
                return v
            names = "abcde"[:len(shape)]
            sizes = {n_: s for n_, s in zip(names[1:], shape[1:])}
            return v.rearrange(f"p ({' '.join(names)}) -> p {' '.join(names)}", **sizes)

        lnp = area(48, [2, D])
        levels_in = area(60, [LEVELS, P])
        qkT = area(0, [2, PAIRS, SEQ])
        vtk = area(16, [NT, HEADS * DH])
        oT = area(24, [PAIRS, SEQ])
        qk_tok = area(32, [NT, HALF])
        rot = area(36, [NT, HALF])
        s_sb = area(40, [4, 384])
        pT = area(56, [2, 384])
        neg_max = area(46, [4, NT])
        row_sum = area(46.125, [4, NT])
        xs = area(0, [NT, 3, DJ, P], BF16, 2)
        res = area(60, [NT, D])
        xeT = area(16, [DJ, CAP])
        pick = area(18, [2, NT, CAP], BF16, 2)
        gpick = area(19, [2, NT, 2, CAP])
        gpT = area(21, [2, NT, P])
        eh = area(23, [SEQ])
        hg = area(24, [SEQ])
        hm = area(25, [2, P])
        hT = area(26, [2, 2, CAP])
        y_e = area(27, [HALF])
        pos = area(29, [NT, NIT])
        gate = area(30.25, [NT, NIT])
        lgT = area(32, [SEQ])
        route_at = 33 * 256

        def scratch(shape, dt=F32):
            nonlocal route_at
            n = int(np.prod(shape)) // (2 if dt == BF16 else 1)
            view = area(route_at / 256, shape, dt, 2 if dt == BF16 else 4)
            route_at += n
            return view

        scores = scratch([NT, NE])
        sel = scratch([NT, NE])
        top = scratch([NT, NG, 8])
        gsum = scratch([NT, 8])
        m8 = scratch([NT, 8])
        i8 = scratch([NT, 8], U32)
        goh = scratch([NT, NG])
        t32 = scratch([NT, NE])
        ing = scratch([NT, EG])
        loh = scratch([NT, 2, EG])
        pair = scratch([NT, EG])
        both = scratch([NT, NE])
        both_b = scratch([NT, NE], BF16)
        gs = scratch([NT])
        cnt = scratch([1])
        gq = area(0, [2, GH, SEQ])
        vtok = area(16, [NC_, GH, GD])
        ktok = area(32, [NC_, 4, GD])
        nlt = area(32, [4, NC_, P])
        tri = area(40, [4, NC_, P])
        ty = area(48, [4, NC_, P])
        triT = area(56, [4, NC_, P])
        att = area(64, [4, NC_, P])
        xc = area(32, [2, 2, TAPS - 1 + SEQ])
        cv = area(37, [2, 2, SEQ])
        ce = area(41, [2, 2, SEQ])
        vT = area(68, [2, NC_, 2, C])
        rn = area(49, [2, 2, SEQ])
        sq = area(64, [2, 2, SEQ])
        gT = area(53, [5, SEQ])
        state = y[:, 0, :].rearrange("p (h d) -> p h d", h=8)
        vnew = area(40, [2, GD])
        vdec = area(41, [2, GD])
        rres = area(42, [2, GD])
        oq = area(43, [2, GD])
        goT = area(0, [2 * GH, SEQ])
        zt = area(40, [4, HALF])
        gcol = sb("gcol", [P, 8, NC_ * GH])
        sdec = sb("sdec", [P, GH, NC_, 2])
        cw = sb("cw", [P, P])
        cw_in = area(58, [P])
        wba = area(58.5, [DJ, 48])
        ab = area(68, [8])
        norm_g = sb("norm_g", [P, GD])
        gcT = sb("gcT", [16, SEQ])
        flag = sb("flag", [P, 2, 2], I32)

        ident_in, const_in, small_in, x_in, ln_in, gdn_in, out_done = (
            sem(n) for n in ("ident_in", "const_in", "small_in", "x_in", "ln_in", "gdn_in", "out_done"))
        slot_full = [sem(f"slot_full{i}") for i in range(RING)]
        init = sem("init")
        own_act, own_dve = sem("own_act"), sem("own_dve")
        x_ready = sem("x_ready")
        xT_ps, xT_sb = sem("xT_ps"), sem("xT_sb")
        y_sb, var_sb, rstd_sb = sem("y_sb"), sem("var_sb"), sem("rstd_sb")
        mix_ps = sem("mix_ps")
        proj_ps, rope_sb, v_sb, tr_ps, qkT_sb = (sem(n) for n in ("proj_ps", "rope_sb", "v_sb", "tr_ps", "qkT_sb"))
        s_ps, s_read, max_sb, exp_sb, p_sb = (sem(n) for n in ("s_ps", "s_read", "max_sb", "exp_sb", "p_sb"))
        pT_ps, pT_sb, o_ps, oT_sb = (sem(n) for n in ("pT_ps", "pT_sb", "o_ps", "oT_sb"))
        lgT_ps, lgT_sb, lg_ps, sc_sb, a_sb, rank_ps = (
            sem(n) for n in ("lgT_ps", "lgT_sb", "lg_ps", "sc_sb", "a_sb", "rank_ps"))
        part_act, left_sb, xs_sb, flag_sb = sem("part_act"), sem("left_sb"), sem("xs_sb"), sem("flag_sb")
        cw_ps, cw_sb = sem("cw_ps"), sem("cw_sb")
        ba_ps, ba_exp, ba_ab, ba_sp, gc_sb, col_ps, col_sb, col_exp = (
            sem(n) for n in ("ba_ps", "ba_exp", "ba_ab", "ba_sp", "gc_sb", "col_ps", "col_sb", "col_exp"))
        cv_ps, xc_sb, cv_sb, ce_sb, si_sb, sq_sb, ss_ps, qk_sb, vt_ps, vt_sb = (
            sem(n) for n in ("cv_ps", "xc_sb", "cv_sb", "ce_sb", "si_sb", "sq_sb", "ss_ps", "qk_sb", "vt_ps", "vt_sb"))
        row_ps, dm_sb, dt_sb, kk_ps, att_sb = (sem(n) for n in ("row_ps", "dm_sb", "dt_sb", "kk_ps", "att_sb"))
        ly_ps, ly_sb, tl_ps, tri_sb, tt_ps, tt_sb = (
            sem(n) for n in ("ly_ps", "ly_sb", "tl_ps", "tri_sb", "tt_ps", "tt_sb"))
        kt_ps, kt_sb, ks_ps, r_sb, oq_sb, tr2_ps, vn_sb, vd_sb, ao_ps, ao_sb, su_ps, st_sb = (
            sem(n) for n in ("kt_ps", "kt_sb", "ks_ps", "r_sb", "oq_sb", "tr2_ps", "vn_sb", "vd_sb", "ao_ps", "ao_sb",
                             "su_ps", "st_sb"))
        tri_init, dec_exp = sem("tri_init"), sem("dec_exp")
        ss_sb, rms_sb = sem("ss_sb"), sem("rms_sb")
        z_ps, z_exp, og_sb, gt_ps, gt_sb = (
            sem(n) for n in ("z_ps", "z_exp", "og_sb", "gt_ps", "gt_sb"))

        class Moe:

            def __init__(self, sems, runs=0, experts=0):
                (self.pick,
                 self.gathered,
                 self.xe,
                 self.gpt,
                 self.w1_used,
                 self.h_ps,
                 self.sig,
                 self.hm,
                 self.hT_ps,
                 self.hT,
                 self.y_ps,
                 self.y,
                 self.own,
                 self.scattered,
                 ) = sems
                self.runs, self.e, self.g = runs, experts, experts + runs
                self.o = (OWN_HEAD - OWN_STEP + OWN_LAST) * runs + OWN_STEP * experts

        def moe_sems(name):
            return [sem(f"{name}_{s}") for s in ("pick", "gathered", "xe", "gpt", "w1_used", "h_ps", "sig", "hm", "hT_ps",
                                                 "hT", "y_ps", "y", "own", "scattered")]

        fast_sems = moe_sems("moe")
        fast = [Moe(fast_sems), Moe(fast_sems, 1, NE)]
        more = [Moe(moe_sems("more0")), Moe(moe_sems("more1"))]
        more_full = [[sem(f"more{layer}_full{i}") for i in range(RING)] for layer in range(2)]

        block = ctx.enter_context(nc.Block())

        def rows(w, cols):
            return w[:, cols].rearrange("(p j) n -> p j n", j=DJ)

        def tiles(w, cols):
            return w[:, cols].rearrange("(c p) n -> p c n", p=P)

        def expert_parts(layer, e):
            w1 = a["moe_w1"][layer, bass.ds(e, 1)].rearrange("a (p j) f -> (a p) j f", j=DJ)
            w3 = a["moe_w3"][layer, bass.ds(e, 1)].rearrange("a (p j) f -> (a p) j f", j=DJ)
            w2 = a["moe_w2"][layer, bass.ds(e, 1)].rearrange("a (h p c) n -> (a p) h (c n)", h=2, c=2)
            return w1, w3, w2

        def w2_view(slot):
            return ring[:, slot].rearrange("p (h q) n -> p h (q n)", h=2).rearrange("p h (c n) -> p h c n", c=2)

        @block.sync
        def _(sp):
            def consumed(u):
                if u < UNIT_ATT + 6:
                    return proj_ps, 2 * (u - UNIT_ATT) + 2
                if u < UNIT_MOE0:
                    return mix_ps, 4
                if u < UNIT_GDN:
                    n, m = divmod(u - UNIT_MOE0, 3)
                    return (fast[0].w1_used, fast[0].h_ps, fast[0].y_ps)[m], n + 1
                u -= UNIT_GDN
                if u < 8:
                    return cv_ps, 2 * u + 2
                if u < 12:
                    return z_ps, 2 * (u - 8) + 2
                return mix_ps, 12

            def load(u, src):
                if u >= RING:
                    sp.wait_ge(*consumed(u - RING))
                sp.dma_start(ring[:, u % RING], src).then_inc(slot_full[u % RING], 16)

            def part(m, slot):
                dst = ring[:, slot]
                return dst.rearrange("p (h q) n -> p h (q n)", h=2) if m == 2 else dst

            def load_experts(layer, u0):
                s = fast[layer]
                for n in range(2):
                    for m, src in enumerate(expert_parts(layer, n)):
                        u = u0 + 3 * n + m
                        sp.wait_ge(*consumed(u - RING))
                        sp.dma_start(part(m, u % RING), src).then_inc(slot_full[u % RING], 16)
                with sp.Fori(1, NE // 2) as i:
                    for b in range(2):
                        for m, src in enumerate(expert_parts(layer, i * 2 + b)):
                            u = u0 + 3 * b + m
                            sp.wait_ge((s.w1_used, s.h_ps, s.y_ps)[m], i * 2 + (b - 1 + s.e))
                            sp.dma_start(part(m, u % RING), src).then_inc(slot_full[u % RING], 16)

            def load_more(layer):
                s = more[layer]
                sp.wait_ge(flag_sb, layer + 1)
                over = sp.value_load(flag[0:1, layer, 0:1])
                with sp.If(over > CAP):
                    sp.wait_ge(fast[layer].y_ps, NE + fast[layer].e)
                    for n in range(2):
                        for m, src in enumerate(expert_parts(layer, n)):
                            sp.dma_start(part(m, 3 * n + m), src).then_inc(more_full[layer][3 * n + m], 16)
                    with sp.Fori(1, (NIT - NE) // 2) as i:
                        for b in range(2):
                            e = (i * 2 + b) % NE
                            for m, src in enumerate(expert_parts(layer, e)):
                                sp.wait_ge((s.w1_used, s.h_ps, s.y_ps)[m], i * 2 + (b - 1 + s.e))
                                sp.dma_start(part(m, 3 * b + m), src).then_inc(more_full[layer][3 * b + m], 16)
                    sp.wait_ge(s.y_ps, NIT - NE)
                with sp.Else():
                    sp.nop()

            sp.dma_start(ident, a["const"][:, 0:P]).then_inc(ident_in, 16)
            sp.dma_start(x[:], a["x"].rearrange("b (t p) d -> p (b t) d", p=P)).then_inc(x_in, 16)
            for g in range(2):
                for w in range(3):
                    if g == 0 and w == 1:
                        sp.dma_start(const[:, P:], a["const"][:, P:]).then_inc(const_in, 16)
                    load(UNIT_ATT + 3 * g + w, rows(a["ab_w_in"][0], slice(w * D + g * HALF, w * D + (g + 1) * HALF)))
            for h in range(2):
                load(UNIT_ATT + 6 + h, tiles(a["ab_w_out"][0], slice(h * HALF, (h + 1) * HALF)))
            load_experts(0, UNIT_MOE0)
            load_more(0)
            for u in range(12):
                load(UNIT_GDN + u, rows(a["gdn_w_in"][0], slice(u * HALF, (u + 1) * HALF)))
            for h in range(2):
                for g in range(2):
                    load(UNIT_GDN + 12 + 2 * h + g,
                         tiles(a["gdn_w_out"][0][g * D:(g + 1) * D], slice(h * HALF, (h + 1) * HALF)))
            load_experts(1, UNIT_MOE1)
            load_more(1)
            for t in range(NT):
                sp.wait_ge(x_ready, 7 + t)
                sp.dma_start(out[0, t * P:(t + 1) * P, :], x[:, t]).then_inc(out_done, 16)
            sp.wait_ge(out_done, 16 * NT)

        @block.gpsimd
        def _(pool):
            def load_ln(n, g, b):
                pool.dma_start(lnp[:, 0], g.partition_broadcast(P)).then_inc(ln_in, 16)
                pool.dma_start(lnp[:, 1], b.partition_broadcast(P)).then_inc(ln_in, 16)

            def parts(layer):
                for t in range(NT):
                    pool.wait_ge(part_act, 4 * layer + t + 1)
                    nc.gpsimd.tensor_tensor(out=res[:, t].rearrange("p (j q) -> p j q", j=DJ),
                                            in0=x[:, t].rearrange("p (q j) -> p j q", j=DJ), in1=xs[:, t, 0],
                                            op=ALU.subtract).then_inc(left_sb, 1)
                for t in range(NT):
                    pool.wait_ge(part_act, 4 * layer + 2 + t + 1)
                    nc.gpsimd.tensor_tensor(out=xs[:, t, 2], in0=res[:, t].rearrange("p (j q) -> p j q", j=DJ),
                                            in1=xs[:, t, 1], op=ALU.subtract).then_inc(xs_sb, 1)

            nc.gpsimd.memset(zeros_b[:], 0.0).then_inc(init, 1)
            nc.gpsimd.memset(flag[:], 0).then_inc(init, 1)
            nc.gpsimd.memset(eps[:], NORM_EPS).then_inc(init, 1)
            load_ln(0, a["mix_ln_g"][0], a["mix_ln_b"][0])
            pool.dma_start(levels_in, a["levels"].rearrange("p (n q) -> p n q", n=LEVELS)).then_inc(small_in, 16)
            pool.dma_start(rw[:], a["router_w"].rearrange("(p j) e -> p j e", j=DJ)).then_inc(small_in, 16)
            pool.dma_start(rbias[:], a["router_bias"].partition_broadcast(P)).then_inc(small_in, 16)
            pool.dma_start(norm_g[:], a["gdn_norm_g"][0].partition_broadcast(P)).then_inc(small_in, 16)
            pool.wait_ge(x_ready, 2)
            load_ln(1, a["ffn_ln_g"][0], a["ffn_ln_b"][0])
            parts(0)
            pool.dma_start(cw_in, a["gdn_conv_w"][0].rearrange("w (c p) -> (w c) p", p=P)).then_inc(gdn_in, 16)
            nc.gpsimd.memset(wba, 0.0).then_inc(init, 1)
            pool.wait_ge(init, 4)
            for i, at in enumerate((0, 32)):
                src = a["gdn_w_in"][0][:, QKV_CH + 2048 + 16 * i:QKV_CH + 2048 + 16 * (i + 1)]
                pool.dma_start(wba[:, :, at:at + 16], src.rearrange("(p j) n -> p j n", j=DJ)).then_inc(gdn_in, 16)
            pool.dma_start(ab[32:48, 0:1], a["gdn_dt_bias"].rearrange("o h -> h o")).then_inc(gdn_in, 16)
            pool.dma_start(ab[32:48, 1:2], a["gdn_a_log"].rearrange("o h -> h o")).then_inc(gdn_in, 16)
            pool.wait_ge(x_ready, 4)
            for n in range(2):
                nc.gpsimd.memset(xc[:, n, :, 0:TAPS - 1], 0.0).then_inc(init, 1)
            pool.wait_ge(ident_in, 16)
            pool.wait_ge(col_ps, 1)
            pool.wait_ge(cw_ps, 1)
            for h in range(GH):
                if h == 4:
                    pool.wait_ge(tr2_ps, 16)
                nc.gpsimd.tensor_copy(triT[:, h % 4], ident.unsqueeze(1).to_broadcast([P, NC_, P])).then_inc(init, 1)
            pool.wait_ge(tl_ps, 2 * (LEVELS - 1) * 4)
            load_ln(2, a["mix_ln_g"][1], a["mix_ln_b"][1])
            pool.wait_ge(x_ready, 6)
            load_ln(3, a["ffn_ln_g"][1], a["ffn_ln_b"][1])
            parts(1)

        @block.tensor
        def _(pe):
            mm, transpose = nc.tensor.matmul, nc.tensor.transpose

            zeros_row = zeros_b[:].unsqueeze(1).to_broadcast([P, 4, P])

            def slot_ready(u):
                pe.wait_ge(slot_full[u % RING], 16 * (u // RING + 1))

            def transpose_x(n):
                for t in range(NT):
                    if n:
                        pe.wait_ge(x_ready, 2 * (n - 1) + 1 + t)
                        pe.wait_ge(mix_ps, 4 * n)
                        pe.wait_ge(y_sb, 2 * n)
                    for b in range(4):
                        for jj in range(2):
                            j = 2 * b + jj
                            last = transpose(psum[b][:, jj * SEQ + t * P:jj * SEQ + (t + 1) * P], x[:, t, j::DJ], ident)
                        if t:
                            last.then_inc(xT_ps, 1)

            def attention():
                pe.wait_ge(x_in, 16)
                pe.wait_ge(ident_in, 16)
                transpose_x(0)
                order = [(0, 0), (0, 1), (0, 2), (1, 0), (1, 1), (1, 2)]
                qk = [n for n in range(6) if order[n][1] < 2]

                def project(n):
                    u = UNIT_ATT + n
                    slot_ready(u)
                    for t in range(NT):
                        if n:
                            if order[n - 1][1] < 2:
                                pe.wait_ge(rope_sb, 2 * qk.index(n - 1) + t + 1)
                            else:
                                pe.wait_ge(v_sb, 2 * (n // 3 - 1) + t + 1)
                        for j in range(DJ):
                            if n == 0:
                                pe.wait_ge(xT_sb, j // 2 + 1)
                            last = mm(psum[4 + t][:], xT[:, j, t * P:(t + 1) * P], ring[:, u % RING, j],
                                      start=(j == 0), stop=(j == DJ - 1))
                        last.then_inc(proj_ps, 1)

                def transpose_qk(n):
                    i = qk.index(n)
                    for t in range(NT):
                        pe.wait_ge(rope_sb, 2 * i + t + 1)
                        if i:
                            pe.wait_ge(qkT_sb, 2 * (i - 1) + t + 1)
                        for q in range(4):
                            last = transpose(psum[6 + t][:, q * P:(q + 1) * P], qk_tok[:, t, q * P:(q + 1) * P], ident)
                        last.then_inc(tr_ps, 1)

                for n in range(6):
                    project(n)
                    if n and order[n - 1][1] < 2:
                        transpose_qk(n - 1)
                pe.wait_ge(qkT_sb, 8)
                pe.wait_ge(v_sb, 4)

                def scores(h):
                    e, pair, bank = h % 2, h // 2, psum[h % 2]
                    if h >= 2:
                        pe.wait_ge(s_read, h - 1)
                    part = slice(e * DH, (e + 1) * DH)
                    mm(bank[:, 0:P], qkT[part, 0, pair, 0:P], qkT[part, 1, pair, 0:P], start=True, stop=True)
                    mm(bank[:, P:3 * P], qkT[part, 0, pair, P:SEQ], qkT[part, 1, pair, :],
                       start=True, stop=True).then_inc(s_ps, 1)

                def transpose_p(h):
                    pe.wait_ge(p_sb, h + 1)
                    if h >= 2:
                        pe.wait_ge(pT_sb, h - 1)
                    for q in range(3):
                        last = transpose(psum[2 + h % 2][:, q * P:(q + 1) * P], s_sb[:, h % 4, q * P:(q + 1) * P], ident)
                    last.then_inc(pT_ps, 1)

                def values(h):
                    e, pair = h % 2, h // 2
                    pe.wait_ge(pT_sb, h + 1)
                    if pair >= 2:
                        pe.wait_ge(oT_sb, pair - 1)
                    o = psum[4 + pair % 2][e * DH:(e + 1) * DH]
                    col = slice(h * DH, (h + 1) * DH)
                    mm(o[:, 0:SEQ], vtk[:, 0, col], pT[:, h % 2, 0:SEQ], start=True, stop=False)
                    mm(o[:, P:SEQ], vtk[:, 1, col], pT[:, h % 2, SEQ:3 * P], start=False, stop=True).then_inc(o_ps, 1)

                for n in range(HEADS + 4):
                    if n < HEADS:
                        scores(n)
                    if 3 <= n < HEADS + 3:
                        transpose_p(n - 3)
                    if n >= 4:
                        values(n - 4)
                pe.wait_ge(oT_sb, PAIRS)
                for h in range(2):
                    slot_ready(UNIT_ATT + 6 + h)
                for t in range(NT):
                    for h in range(2):
                        u = UNIT_ATT + 6 + h
                        for c in range(PAIRS):
                            last = mm(psum[2 * h + t][:], oT[:, c, t * P:(t + 1) * P], ring[:, u % RING, c],
                                      start=(c == 0), stop=(c == PAIRS - 1))
                        last.then_inc(mix_ps, 1)

            def router(layer):
                pe.wait_ge(small_in, 64)
                transpose_x(1 + 2 * layer)
                for j in range(DJ):
                    pe.wait_ge(xT_sb, 4 * (1 + 2 * layer) + j // 2 + 1)
                    last = mm(psum[4][0:NE, 0:SEQ], rw[:, j], xT[:, j], start=(j == 0), stop=(j == DJ - 1))
                last.then_inc(lgT_ps, 1)
                pe.wait_ge(lgT_sb, layer + 1)
                for t in range(NT):
                    last = transpose(psum[5][:, t * NE:(t + 1) * NE], lgT[0:NE, t * P:(t + 1) * P], ident[0:NE, 0:NE])
                last.then_inc(lg_ps, 1)
                for t in range(NT):
                    for h in range(2):
                        mm(psum[2 * h + t][:], k("alpha"), x[:, t, h * HALF:(h + 1) * HALF], start=True, stop=False)
                pe.wait_ge(a_sb, layer + 1)
                r = psum[6]
                mm(r[:, 0:NE], upper_b[:], both_b[:, 0], start=True, stop=True)
                mm(r[:, NE:2 * NE], ones_b[:], both_b[:, 0], start=True, stop=False)
                mm(r[:, NE:2 * NE], upper_b[:], both_b[:, 1], start=False, stop=True)
                mm(r[:, 2 * NE:3 * NE], ones_b[:], both_b[:, 0], start=True, stop=False)
                mm(r[:, 2 * NE:3 * NE], ones_b[:], both_b[:, 1], start=False, stop=True).then_inc(rank_ps, 1)

            def gather(s, b, wait):
                pe.wait_ge(s.pick, wait + s.e)
                for j in range(DJ):
                    for t in range(NT):
                        for part in range(3):
                            mm(psum[4][:, j * CAP:(j + 1) * CAP], xs[:, t, part, j], pick[:, b, t],
                               start=(t == 0 and part == 0), stop=(t == NT - 1 and part == 2))
                for t in range(NT):
                    last = transpose(psum[5][:, t * P:(t + 1) * P],
                                     gpick[:, b, t].rearrange("p d s -> p (d s)"), ident)
                last.then_inc(s.gathered, 1)

            def scatter(s, b, wait):
                pe.wait_ge(s.y, wait + s.g)
                pe.wait_ge(s.gpt, wait + s.g)
                for t in range(NT):
                    for h in range(2):
                        part = slice(h * CAP, (h + 1) * CAP)
                        last = mm(psum[2 * h + t][:], gpT[part, b, t], y_e[part], start=False, stop=False,
                                  skip_group_check=True)
                return last

            def experts(s, fulls, steps, first):
                def turn(i, ends):
                    for b in range(2):
                        n = i * 2 + b
                        slots = [(first + 3 * b + m) % RING for m in range(3)]
                        filled = [i * 16 + 16 * ((first + 3 * b + m) // RING + 1) for m in range(3)]
                        pe.wait_ge(s.xe, n + (1 + s.e))
                        pe.wait_ge(s.gpt, n + (2 + s.g))
                        for m in range(2):
                            pe.wait_ge(fulls[slots[m]], filled[m])
                            for j in range(DJ):
                                for h in range(2):
                                    last = mm(psum[5][h * CAP:(h + 1) * CAP, m * SEQ:(m + 1) * SEQ], xeT[:, j],
                                              ring[:, slots[m], j, h * SEQ:(h + 1) * SEQ],
                                              start=(j == 0), stop=(j == DJ - 1))
                            last.then_inc((s.w1_used, s.h_ps)[m], 1)
                        scatter(s, 1 - b, n + 1)
                        pe.wait_ge(s.hm, n + (1 + s.e))
                        for c in range(2):
                            last = transpose(psum[6][:, c * P:(c + 1) * P], hm[:, c], ident)
                        last.then_inc(s.hT_ps, 1)
                        if not (ends and b):
                            gather(s, 1 - b, n + 2)
                        pe.wait_ge(s.hT, n + (1 + s.e))
                        pe.wait_ge(fulls[slots[2]], filled[2])
                        w2 = w2_view(slots[2])
                        for g in range(2):
                            for c in range(2):
                                for h in range(2):
                                    last = mm(psum[7][h * CAP:(h + 1) * CAP], hT[:, c, g],
                                              w2[:, g, c, h * HALF:(h + 1) * HALF],
                                              start=(g == 0 and c == 0), stop=(g == 1 and c == 1))
                        last.then_inc(s.y_ps, 1)

                gather(s, 0, 1)
                with pe.Fori(0, steps // 2 - 1) as i:
                    turn(i, False)
                turn(steps // 2 - 1, True)
                scatter(s, 1, steps + 1).then_inc(s.scattered, 1)

            def moe(layer, u0):
                router(layer)
                pe.wait_ge(xs_sb, 2 * (layer + 1))
                pe.wait_ge(flag_sb, layer + 1)
                experts(fast[layer], slot_full, NE, u0)
                over = pe.value_load(flag[0:1, layer, 0:1])
                with pe.If(over > CAP):
                    experts(more[layer], more_full[layer], NIT - NE, 0)
                with pe.Else():
                    pe.nop()
                for b in (0, 2, 1, 3):
                    mm(psum[b][:], zeros_b[:], zeros_row, start=False, stop=True).then_inc(mix_ps, 1)

            def gdn():
                transpose_x(2)
                def project(n):
                    if n >= 2:
                        pe.wait_ge(xc_sb, n - 1)
                    for i in range(2):
                        ch = 2 * n + i
                        u = UNIT_GDN + ch // 4
                        if ch % 4 == 0:
                            slot_ready(u)
                        for j in range(DJ):
                            if n == 0 and i == 0:
                                pe.wait_ge(xT_sb, 8 + j // 2 + 1)
                            last = mm(psum[n % 2][:, i * SEQ:(i + 1) * SEQ],
                                      ring[:, u % RING, j, (ch % 4) * P:(ch % 4 + 1) * P], xT[:, j],
                                      start=(j == 0), stop=(j == DJ - 1))
                    last.then_inc(cv_ps, 1)

                def squares(m):
                    pe.wait_ge(sq_sb, m + 1)
                    if m >= 2:
                        pe.wait_ge(ss_sb, m // 2 * 2)
                    mm(psum[2 + 2 * (m % 2)][:], k("ones"), sq[:, m % 2].rearrange("p a b -> p (a b)"), start=True,
                       stop=True).then_inc(ss_ps, 1)

                def v_tokens(m):
                    h = m - 8
                    pe.wait_ge(si_sb, m + 1)
                    if h >= 2:
                        pe.wait_ge(vt_sb, h - 1)
                    for c in range(NC_):
                        last = transpose(psum[6 + m % 2][:, c * P:(c + 1) * P],
                                         vT[:, m % 2, c].rearrange("p e i -> p (e i)"), ident)
                    last.then_inc(vt_ps, 1)

                def decay_rows(half):
                    for n in range(4):
                        h = 4 * half + n
                        bank = psum[ROW_BANKS[half] + n][:].rearrange("p (c e i) -> p c e i", c=NC_, e=2)
                        for e in range(2):
                            last = mm(bank[:, :, e], ident[0:16, 2 * h + e:2 * h + e + 1].to_broadcast([16, P]),
                                      gcT[:], start=True, stop=True)
                        last.then_inc(row_ps, 1)

                def products(half, n):
                    h = 4 * half + n
                    for c in range(NC_):
                        for e in range(2):
                            last = mm(psum[4 + n][e * C:(e + 1) * C, c * P:(c + 1) * P],
                                      gq[:, 1, h, c * C:(c + 1) * C], gq[:, :, h, c * C:(c + 1) * C],
                                      start=True, stop=True)
                    last.then_inc(kk_ps, 1)

                for n in range(18):
                    if n < 16:
                        project(n)
                    if n == 17:
                        pe.wait_ge(qk_sb, 8)
                        pe.wait_ge(dt_sb, 8)
                        products(0, 0)
                        products(0, 1)
                        pe.wait_ge(vt_sb, 7)
                        products(0, 2)
                    if n == 0:
                        pe.wait_ge(gdn_in, 80)
                        transpose(psum[7][:, 0:P], cw_in, ident).then_inc(cw_ps, 1)
                        for j in range(DJ):
                            last = mm(psum[3][0:48, 0:SEQ], wba[:, j], xT[:, j], start=(j == 0), stop=(j == DJ - 1))
                        last.then_inc(ba_ps, 1)
                    if n == 11:
                        pe.wait_ge(ss_sb, 8)
                        pe.wait_ge(col_sb, 1)
                        decay_rows(0)
                    if 3 <= n < 11:
                        squares(n - 3)
                    if n >= 10:
                        v_tokens(n - 2)
                    if n == 4:
                        pe.wait_ge(gc_sb, 1)
                        for w in range(2):
                            src = gT[0:16, 2] if w else gcT[:]
                            for c in range(NC_):
                                for e in range(2):
                                    last = mm(psum[3][e * C:(e + 1) * C, (w * NC_ + c) * GH:(w * NC_ + c + 1) * GH],
                                              src[:, c * C:(c + 1) * C], ident[0:16, e:16:2], start=True, stop=True)
                        last.then_inc(col_ps, 1)
                pe.wait_ge(vt_sb, 8)
                products(0, 3)
                for half in range(2):
                    if half:
                        pe.wait_ge(oq_sb, 12)
                        pe.wait_ge(ao_sb, 16)
                    if half:
                        for n in range(4):
                            products(half, n)
                    for n in range(4):
                        pe.wait_ge(tri_init, 4 * half + n + 1)
                        for c in range(NC_):
                            last = transpose(psum[n][:, c * P:(c + 1) * P], triT[:, n, c], ident)
                        last.then_inc(tt_ps, 1)
                    for lv in range(1, LEVELS):
                        for n in range(4):
                            g = (half * (LEVELS - 1) + lv - 1) * 4 + n
                            pe.wait_ge(tt_sb, g + 1)
                            for c in range(NC_):
                                last = mm(psum[n][:, c * P:(c + 1) * P], nlt[:, n, c], tri[:, n, c], start=True, stop=True)
                            last.then_inc(ly_ps, 1)
                        for n in range(4):
                            g = (half * (LEVELS - 1) + lv - 1) * 4 + n
                            pe.wait_ge(ly_sb, g + 1)
                            if lv == 1:
                                pe.wait_ge(att_sb, 4 * half + n + 1)
                            for c in range(NC_):
                                left, right = (ty, triT) if lv == LEVELS - 1 else (triT, ty)
                                last = mm(psum[4 + n][:, c * P:(c + 1) * P], left[:, n, c], right[:, n, c], start=True,
                                          stop=True)
                            last.then_inc(tl_ps, 1)
                        if lv < LEVELS - 1:
                            for n in range(4):
                                g = (half * (LEVELS - 1) + lv - 1) * 4 + n
                                pe.wait_ge(tri_sb, g + 1)
                                for c in range(NC_):
                                    last = transpose(psum[n][:, c * P:(c + 1) * P], tri[:, n, c], ident)
                                last.then_inc(tt_ps, 1)
                    if half == 0:
                        pe.wait_ge(tri_sb, (LEVELS - 1) * 4)
                        decay_rows(1)
                    for n in range(4):
                        for c in range(NC_):
                            for e in range(2):
                                last = mm(psum[n][e * C:(e + 1) * C, c * P:(c + 1) * P],
                                          gq[:, 1, 4 * half + n, c * C:(c + 1) * C], ident, start=True, stop=True)
                        last.then_inc(kt_ps, 1)
                    pe.wait_ge(kt_sb, 4 * half + 4)
                    pe.wait_ge(tri_sb, (half + 1) * (LEVELS - 1) * 4)

                    def read_state(g):
                        c, n = g // 4, g % 4
                        h = 4 * half + n
                        G = half * 16 + g
                        if c == 0:
                            return
                        pe.wait_ge(st_sb, half * 12 + 4 * (c - 1) + n + 1)
                        if g >= 6:
                            pe.wait_ge(r_sb, G - 1)
                            pe.wait_ge(oq_sb, half * 12 + g - 4 - 1)
                        bank = psum[g % 2]
                        for w in (1, 0):
                            for e in range(2):
                                last = mm(bank[e * C:(e + 1) * C, w * P:(w + 1) * P], gq[:, w, h, c * C:(c + 1) * C],
                                          state[:, 2 * n + e], start=True, stop=True)
                        last.then_inc(ks_ps, 1)

                    def solve(g):
                        c, n = g // 4, g % 4
                        G = half * 16 + g
                        if c:
                            pe.wait_ge(r_sb, G + 1)
                        if g >= 2:
                            pe.wait_ge(vd_sb, G - 1)
                            pe.wait_ge(vn_sb, G - 1)
                        rhs = rres[:, g % 2] if c else vtok[:, 0, 4 * half + n]
                        mm(psum[2 + g % 2][:, 0:P], triT[:, n, c], rhs, start=True, stop=True).then_inc(tr2_ps, 1)

                    def finish(g):
                        c, n = g // 4, g % 4
                        G = half * 16 + g
                        pe.wait_ge(vn_sb, G + 1)
                        if g >= 2:
                            pe.wait_ge(ao_sb, G - 1)
                        elif half == 0:
                            pe.wait_ge(dt_sb, 16)
                        mm(psum[4 + g % 2][:, 0:P], att[:, n, c], vnew[:, g % 2], start=True, stop=True).then_inc(ao_ps, 1)
                        if c < NC_ - 1:
                            pe.wait_ge(vd_sb, G + 1)
                            if g >= 1:
                                pe.wait_ge(st_sb, half * 12 + g)
                            for e in range(2):
                                part = slice(e * C, (e + 1) * C)
                                last = mm(psum[6 + e][:, 0:P], ktok[part, c, n], vdec[part, g % 2], start=True, stop=True)
                            last.then_inc(su_ps, 1)

                    for g in range(18):
                        if g < 16:
                            read_state(g)
                        if 1 <= g <= 16:
                            solve(g - 1)
                        if g >= 2:
                            finish(g - 2)
                for zz in range(4):
                    u = UNIT_GDN + 8 + zz
                    slot_ready(u)
                    w = ring[:, u % RING].rearrange("p j (h e d) -> p j h e d", h=2, e=2)
                    for cp in range(2):
                        i = 2 * zz + cp
                        if i >= 4:
                            pe.wait_ge(og_sb, i - 3)
                        else:
                            pe.wait_ge(ao_sb, 32)
                        for cc in range(2):
                            c = 2 * cp + cc
                            for j in range(DJ):
                                for e in range(2):
                                    last = mm(psum[Z_BANKS[i % 4]][e * C:(e + 1) * C, cc * SEQ:(cc + 1) * SEQ],
                                              xT[:, j, c * C:(c + 1) * C], w[:, j, :, e], start=(j == 0), stop=(j == DJ - 1))
                        last.then_inc(z_ps, 1)
                        if i >= 2:
                            gated_transpose(i - 2)
                gated_transpose(6)
                gated_transpose(7)
                pe.wait_ge(gt_sb, 8)
                for u in range(UNIT_GDN + 12, UNIT_GDN + 16):
                    slot_ready(u)
                for t in range(NT):
                    for h in range(2):
                        for c in range(2 * GH):
                            u = UNIT_GDN + 12 + 2 * h + c // 8
                            last = mm(psum[2 * h + t][:], goT[:, c, t * P:(t + 1) * P], ring[:, u % RING, c % 8],
                                      start=(c == 0), stop=(c == 2 * GH - 1))
                        last.then_inc(mix_ps, 1)

            def gated_transpose(i):
                zz, cp = i // 2, i % 2
                pe.wait_ge(og_sb, i + 1)
                if i >= 2:
                    pe.wait_ge(gt_sb, i - 1)
                for hh in range(2):
                    for cc in range(2):
                        last = transpose(psum[2 + i % 2][:, (2 * hh + cc) * P:(2 * hh + cc + 1) * P],
                                         vtok[:, 2 * cp + cc, 2 * zz + hh], ident)
                last.then_inc(gt_ps, 1)

            attention()
            moe(0, UNIT_MOE0)
            gdn()
            moe(1, UNIT_MOE1)

        @block.scalar
        def _(act):
            do = nc.scalar.activation
            own = Own(act, own_act)

            def copy(o, i, **kw):
                return do(o, i, ACT.Copy, **kw)

            def inverse_root(n):
                for t in range(NT):
                    var, r = spread[:, t, 0:1], spread[:, t, 1:2]
                    act.wait_ge(var_sb, 2 * n + t + 1)
                    own.link(do(r, var, ACT.Ln))
                    do(r, r, ACT.Exp, scale=-0.5).then_inc(rstd_sb, 1)

            def evacuate_xT(n):
                for b in range(4):
                    act.wait_ge(xT_ps, 4 * n + b + 1)
                    copy(xT[:, 2 * b:2 * b + 2], psum[b][:].rearrange("p (j t) -> p j t", j=2)).then_inc(xT_sb, 1)

            def attention():
                evacuate_xT(0)

                def evacuate_qkT(i):
                    g, w = i // 2, i % 2
                    for t in range(NT):
                        act.wait_ge(tr_ps, 2 * i + t + 1)
                        copy(qkT[:, w, 4 * g:4 * g + 4, t * P:(t + 1) * P],
                             psum[6 + t][:].rearrange("p (q t) -> p q t", q=4)).then_inc(qkT_sb, 1)

                for g in range(2):
                    evacuate_qkT(2 * g)
                    for t in range(NT):
                        act.wait_ge(proj_ps, 6 * g + 4 + t + 1)
                        copy(vtk[:, t, g * HALF:(g + 1) * HALF], psum[4 + t][:]).then_inc(v_sb, 1)
                    evacuate_qkT(2 * g + 1)
                for n in range(HEADS + 4):
                    if n < HEADS:
                        act.wait_ge(max_sb, n + 1)
                        b = n % 4
                        do(s_sb[:, b, 0:P], s_sb[:, b, 0:P], ACT.Exp, scale=-1.0, bias=neg_max[:, b, 0:1],
                           accum_out=row_sum[:, b, 0:1]).then_inc(exp_sb, 1)
                        do(s_sb[:, b, P:3 * P], s_sb[:, b, P:3 * P], ACT.Exp, scale=-1.0, bias=neg_max[:, b, 1:2],
                           accum_out=row_sum[:, b, 1:2]).then_inc(exp_sb, 1)
                    if 3 <= n < HEADS + 3:
                        m = n - 3
                        act.wait_ge(pT_ps, m + 1)
                        if m >= 2:
                            act.wait_ge(o_ps, m - 1)
                        copy(pT[:, m % 2], psum[2 + m % 2][:, 0:384]).then_inc(pT_sb, 1)
                    if n >= 5 and n % 2:
                        pair = (n - 5) // 2
                        act.wait_ge(o_ps, 2 * pair + 2)
                        copy(oT[:, pair], psum[4 + pair % 2][:, 0:SEQ]).then_inc(oT_sb, 1)

            def moe(layer):
                evacuate_xT(1 + 2 * layer)
                for t in range(NT):
                    act.wait_ge(x_ready, 4 * layer + 1 + t)
                    copy(xs[:, t, 0], x[:, t].rearrange("p (q j) -> p j q", j=DJ)).then_inc(part_act, 1)
                act.wait_ge(lgT_ps, layer + 1)
                copy(lgT[0:NE], psum[4][0:NE, 0:SEQ]).then_inc(lgT_sb, 1)
                act.wait_ge(lg_ps, layer + 1)
                do(scores.rearrange("p t e -> p (t e)"), psum[5][:, 0:NT * NE], ACT.Exp, scale=-1.0).then_inc(sc_sb, 1)
                for t in range(NT):
                    act.wait_ge(left_sb, 2 * layer + t + 1)
                    copy(xs[:, t, 1], res[:, t].rearrange("p (j q) -> p j q", j=DJ)).then_inc(part_act, 1)

                def experts(s, steps):
                    with act.Fori(0, steps) as n:
                        act.wait_ge(s.gathered, n + (1 + s.e))
                        copy(xeT.rearrange("p j s -> p (j s)"), psum[4][:]).then_inc(s.xe, 1)
                        act.wait_ge(s.h_ps, n + (1 + s.e))
                        do(eh, psum[5][:, 0:SEQ], ACT.Tanh, scale=0.5).then_inc(s.sig, 1)
                        act.wait_ge(s.hT_ps, n + (1 + s.e))
                        copy(hT.rearrange("p c g s -> p (c g s)"), psum[6][:, 0:SEQ]).then_inc(s.hT, 1)

                act.wait_ge(flag_sb, layer + 1)
                experts(fast[layer], NE)
                over = act.value_load(flag[0:1, layer, 0:1])
                with act.If(over > CAP):
                    experts(more[layer], NIT - NE)
                with act.Else():
                    act.nop()

            def gdn():
                evacuate_xT(2)

                def decays(half, n):
                    h = 4 * half + n
                    rowv = psum[ROW_BANKS[half] + n][:].rearrange("p (c e i) -> p c e i", c=NC_, e=2)
                    act.wait_ge(dm_sb, h + 1)
                    do(sdec[:, h], rowv[:, :, :, C - 1], ACT.Exp).then_inc(dt_sb, 1)
                    do(ty[:, n], ty[:, n], ACT.Exp).then_inc(dt_sb, 1)
                    if n == 3:
                        dec = gcol[:, 5].rearrange("p (c h) -> p c h", h=GH)[:, :, 4 * half:4 * half + 4]
                        do(dec, dec, ACT.Exp).then_inc(dec_exp, 1)

                for n in range(18):
                    if 1 <= n <= 16:
                        act.wait_ge(cv_sb, n)
                        if n >= 3:
                            act.wait_ge(si_sb, n - 2)
                        do(ce[:, (n - 1) % 2], cv[:, (n - 1) % 2], ACT.Tanh, scale=0.5).then_inc(ce_sb, 1)
                    if n < 16:
                        act.wait_ge(cv_ps, n + 1)
                        if n >= 2:
                            act.wait_ge(cv_sb, n - 1)
                        else:
                            act.wait_ge(init, 6)
                        copy(xc[:, n % 2, :, TAPS - 1:], psum[n % 2][:].rearrange("p (i t) -> p i t", i=2)
                             ).then_inc(xc_sb, 1)
                    if n == 0:
                        act.wait_ge(cw_ps, 1)
                        copy(cw[:], psum[7][:, 0:P]).then_inc(cw_sb, 1)
                        act.wait_ge(ba_ps, 1)
                        do(gT[0:16, 4], psum[3][0:16, 0:SEQ], ACT.Exp, scale=-1.0).then_inc(ba_exp, 1)
                        do(ab[32:48, 2:3], ab[32:48, 1:2], ACT.Exp).then_inc(ba_exp, 1)
                        act.wait_ge(ba_ab, 1)
                        own.link(do(gT[32:48, 1], gT[32:48, 1], ACT.Exp))
                        do(gT[32:48, 1], gT[32:48, 1], ACT.Ln, bias=1.0).then_inc(ba_sp, 1)
                    if 2 <= n < 10:
                        m = n - 2
                        act.wait_ge(si_sb, m + 1)
                        if m >= 2:
                            act.wait_ge(ss_ps, m - 1)
                        do(sq[:, m % 2], gq[:, m // 4, 2 * (m % 4):2 * (m % 4) + 2], ACT.Square).then_inc(sq_sb, 1)
                    if 4 <= n < 12 and n % 2 == 0:
                        m = n - 4
                        if m:
                            act.wait_ge(qk_sb, m)
                        for i in range(2):
                            act.wait_ge(ss_ps, m + i + 1)
                            own(do(rn[:, i].rearrange("p a b -> p (a b)"), psum[2 + 2 * i][:], ACT.Ln, bias=eps[:],
                                   scale=0.25))
                        own.wait()
                        for i in range(2):
                            do(rn[:, i], rn[:, i], ACT.Exp, scale=-0.5).then_inc(ss_sb, 1)
                    if n == 5:
                        act.wait_ge(col_sb, 1)
                        do(gcol[:, 2], gcol[:, 0], ACT.Exp).then_inc(col_exp, 1)
                    if 12 <= n < 16:
                        decays(0, n - 12)
                    if n >= 10:
                        h = n - 10
                        act.wait_ge(vt_ps, h + 1)
                        copy(vtok[:, :, h], psum[6 + h % 2][:].rearrange("p (c d) -> p c d", c=NC_),
                             scale=0.5).then_inc(vt_sb, 1)
                for half in range(2):
                    for lv in range(LEVELS):
                        for n in range(4 if lv else 0):
                            act.wait_ge(ly_ps, (half * (LEVELS - 1) + lv - 1) * 4 + n + 1)
                            if lv == 1:
                                act.wait_ge(att_sb, 4 * half + n + 1)
                            copy(ty[:, n].rearrange("p c i -> p (c i)"), psum[n][:]).then_inc(ly_sb, 1)
                        for n in range(4 if lv < LEVELS - 1 else 0):
                            act.wait_ge(tt_ps, (half * (LEVELS - 1) + lv) * 4 + n + 1)
                            dst = triT if lv else tri
                            copy(dst[:, n].rearrange("p c i -> p (c i)"), psum[n][:]).then_inc(tt_sb, 1)
                    for n in range(4):
                        if half == 0:
                            decays(1, n)
                        act.wait_ge(kt_ps, 4 * half + n + 1)
                        copy(ktok[:, :, n], psum[n][:].rearrange("p (c d) -> p c d", c=NC_)).then_inc(kt_sb, 1)
                    for g in range(17):
                        G = half * 16 + g
                        c, n = g // 4, g % 4
                        u = c * GH + 4 * half + n
                        if g >= 1:
                            g1 = g - 1
                            G1 = G - 1
                            c, n = g1 // 4, g1 % 4
                            u = c * GH + 4 * half + n
                            act.wait_ge(tr2_ps, G1 + 1)
                            if g1 >= 2:
                                act.wait_ge(ao_ps, G1 - 1)
                                act.wait_ge(vd_sb, G1 - 1)
                            copy(vnew[:, g1 % 2], psum[2 + g1 % 2][:, 0:P], scale=gcol[:, 1, u:u + 1]).then_inc(vn_sb, 1)
                        if g < 16 and g >= 4:
                            u = g // 4 * GH + 4 * half + g % 4
                            act.wait_ge(r_sb, G + 1)
                            if g >= 6:
                                act.wait_ge(ao_sb, G - 1)
                            copy(oq[:, g % 2], psum[g % 2][:, 0:P], scale=gcol[:, 3, u:u + 1]).then_inc(oq_sb, 1)
                act.wait_ge(ao_sb, 32)
                for u in range(32):
                    c, h = u // GH, u % GH
                    if u:
                        own.wait()
                    own(do(zt[:, 0, 0:P], vtok[:, c, h], ACT.Square, accum_out=gcol[:, 7, u:u + 1]))
                own.wait()
                own.link(do(gcol[:, 7], gcol[:, 7], ACT.Ln, bias=eps[:], scale=1.0 / GD))
                do(gcol[:, 7], gcol[:, 7], ACT.Exp, scale=-0.5).then_inc(rms_sb, 1)
                for i in range(10):
                    if i < 8:
                        act.wait_ge(z_ps, i + 1)
                        if i >= 4:
                            act.wait_ge(og_sb, i - 3)
                        do(zt[:, i % 4], psum[Z_BANKS[i % 4]][:], ACT.Tanh, scale=0.5).then_inc(z_exp, 1)
                    if i >= 2:
                        m = i - 2
                        zz, cp = m // 2, m % 2
                        act.wait_ge(gt_ps, m + 1)
                        for hh in range(2):
                            dst = goT[:, 2 * (2 * zz + hh):2 * (2 * zz + hh) + 2, 2 * cp * C:2 * (cp + 1) * C]
                            ins = copy(dst.rearrange("p e (c i) -> p c e i", c=2),
                                       psum[2 + m % 2][:, 2 * hh * P:2 * (hh + 1) * P].rearrange(
                                           "p (c e i) -> p c e i", c=2, e=2))
                            if hh:
                                ins.then_inc(gt_sb, 1)
                            else:
                                own(ins)

            attention()
            inverse_root(0)
            moe(0)
            inverse_root(1)
            gdn()
            inverse_root(2)
            moe(1)
            inverse_root(3)

        @block.vector
        def _(dve):
            v = nc.vector
            own = Own(dve, own_dve)

            def layer_norm(n):
                def summed(t, h):
                    return psum[2 * h + t][:] if n % 2 else y[:, t, h * HALF:(h + 1) * HALF]

                def gained(t):
                    for h in range(2):
                        col = slice(h * HALF, (h + 1) * HALF)
                        ins = v.scalar_tensor_tensor(out=y[:, t, col], in0=summed(t, h), scalar=mv[:, t, 0:1],
                                                     in1=lnp[:, 0, col], op0=ALU.subtract, op1=ALU.mult)
                        if n % 2 and h:
                            ins.then_inc(y_sb, 1)
                            dve.wait_ge(y_sb, 2 * n + t + 1)
                        else:
                            own(ins)

                def scaled(t):
                    var, r, w = (spread[:, t, i:i + 1] for i in range(3))
                    dve.wait_ge(rstd_sb, 2 * n + t + 1)
                    own.link(v.tensor_tensor(out=w, in0=r, in1=r, op=ALU.mult))
                    own.link(v.tensor_tensor(out=w, in0=w, in1=var, op=ALU.mult))
                    own.link(v.tensor_scalar(out=w, in0=w, scalar1=-0.5, scalar2=1.5, op0=ALU.mult, op1=ALU.add))
                    own.link(v.tensor_tensor(out=r, in0=r, in1=w, op=ALU.mult))
                    v.scalar_tensor_tensor(out=x[:, t], in0=y[:, t], scalar=r, in1=lnp[:, 1], op0=ALU.mult,
                                           op1=ALU.add).then_inc(x_ready, 1)

                dve.wait_ge(ln_in, 32 * (n + 1))
                for t in range(NT):
                    for h in range(2):
                        dve.wait_ge(mix_ps, 4 * n + (4 if n % 2 else 2 * t + h + 1))
                        col = slice(h * HALF, (h + 1) * HALF)
                        if n % 2 == 0:
                            ins = v.scalar_tensor_tensor(out=y[:, t, col], in0=x[:, t, col], scalar=ALPHA,
                                                         in1=psum[2 * h + t][:], op0=ALU.mult, op1=ALU.add)
                            if h:
                                ins.then_inc(y_sb, 1)
                                dve.wait_ge(y_sb, 2 * n + t + 1)
                            else:
                                own.link(ins)
                        own(v.bn_stats(stats[:, t, h], summed(t, h)))
                    own.wait()
                    own.link(v.bn_aggr(mv[:, t], stats[:, t]))
                    v.tensor_scalar(out=spread[:, t, 0:1], in0=mv[:, t, 1:2], scalar1=LN_EPS, scalar2=None,
                                    op0=ALU.add).then_inc(var_sb, 1)
                    gained(t)
                    if t == 0 and n % 2 == 0:
                        own.wait()
                        scaled(0)
                own.wait()
                for t in range(NT if n % 2 else 1):
                    scaled(t if n % 2 else 1)

            def attention():
                dve.wait_ge(const_in, 16)
                cos = k("cos").rearrange("p (t a h d) -> p t a h d", t=NT, a=1, h=1)
                sin = k("sin").rearrange("p (t a h d) -> p t a h d", t=NT, a=1, h=1)
                i = 0
                for n in range(6):
                    if n % 3 == 2:
                        continue
                    for t in range(NT):
                        dve.wait_ge(proj_ps, 2 * n + t + 1)
                        if i >= 2:
                            dve.wait_ge(tr_ps, i - 1)
                        src = psum[4 + t][:].rearrange("p (a d) -> p a d", d=32)
                        o4 = qk_tok[:, t].rearrange("p (a h d) -> p a h d", h=2, d=32)
                        o3 = qk_tok[:, t].rearrange("p (a d) -> p a d", d=32)
                        r4 = rot[:, t].rearrange("p (a h d) -> p a h d", h=2, d=32)
                        r3 = rot[:, t].rearrange("p (a d) -> p a d", d=32)
                        cb = cos[:, t, 0].to_broadcast([P, 16, 32])
                        sb_ = sin[:, t, 0].to_broadcast([P, 16, 32])
                        own(v.tensor_tensor(out=o3, in0=src, in1=cb, op=ALU.mult))
                        own.link(v.tensor_tensor(out=r3, in0=src, in1=sb_, op=ALU.mult))
                        own(v.tensor_tensor(out=o4[:, :, 0], in0=o4[:, :, 0], in1=r4[:, :, 1], op=ALU.subtract))
                        own.link(v.tensor_tensor(out=o4[:, :, 1], in0=o4[:, :, 1], in1=r4[:, :, 0], op=ALU.add))
                        dve.sem_inc(rope_sb, 1)
                        i += 1
                dve.wait_ge(small_in, 64)
                own(v.tensor_copy(upper_b[:], k("upper")))
                own(v.tensor_copy(ones_b[:], k("ones")))
                own(v.tensor_copy(levels[:], levels_in))
                for n in range(HEADS + 2):
                    if n < HEADS:
                        b = n % 4
                        dve.wait_ge(s_ps, n + 1)
                        if n >= 4:
                            dve.wait_ge(pT_ps, n - 3)
                        v.scalar_tensor_tensor(out=s_sb[:, b], in0=psum[n % 2][:, 0:384], scalar=-ATT_SCALE,
                                               in1=k("mask_a" if n < 8 else "mask_b"), op0=ALU.mult,
                                               op1=ALU.subtract).then_inc(s_read, 1)
                        dve.wait_ge(s_read, n + 1)
                        own(v.tensor_reduce(out=neg_max[:, b, 0:1], in_=s_sb[:, b, 0:P], axis=AX, op=ALU.min))
                        own.link(v.tensor_reduce(out=neg_max[:, b, 1:2], in_=s_sb[:, b, P:384], axis=AX, op=ALU.min))
                        dve.sem_inc(max_sb, 1)
                    if n >= 2:
                        m = n - 2
                        b = m % 4
                        dve.wait_ge(exp_sb, 2 * m + 2)
                        own.link(v.reciprocal(row_sum[:, b], row_sum[:, b]))
                        own(v.tensor_scalar(out=s_sb[:, b, 0:P], in0=s_sb[:, b, 0:P], scalar1=row_sum[:, b, 0:1],
                                            scalar2=None, op0=ALU.mult))
                        own.link(v.tensor_scalar(out=s_sb[:, b, P:384], in0=s_sb[:, b, P:384], scalar1=row_sum[:, b, 1:2],
                                                 scalar2=None, op0=ALU.mult))
                        dve.sem_inc(p_sb, 1)
                layer_norm(0)

            def route(layer):
                iota = k("iota")

                def over(view, n, at):
                    view = view.unsqueeze(at)
                    shape = list(view.shape)
                    shape[at] = n
                    return view.to_broadcast(shape)

                own(v.memset(gsum, NEG))
                dve.wait_ge(sc_sb, layer + 1)
                own.link(v.tensor_scalar(out=scores, in0=scores, scalar1=1.0, scalar2=None, op0=ALU.add))
                own.link(v.reciprocal(scores, scores))
                own.link(v.tensor_tensor(out=sel, in0=scores, in1=over(rbias[:], NT, 1), op=ALU.add))
                for t in range(NT):
                    for g in range(NG):
                        own(v.max(out=top[:, t, g], in_=sel[:, t, g * EG:(g + 1) * EG]))
                own.wait()
                own.link(v.tensor_tensor(out=gsum[:, :, 0:NG], in0=top[:, :, :, 0], in1=top[:, :, :, 1], op=ALU.add))
                for t in range(NT):
                    own(v.max(out=m8[:, t], in_=gsum[:, t]))
                own.wait()
                for t in range(NT):
                    own(v.max_index(out=i8[:, t], in_max=m8[:, t], in_values=gsum[:, t]))
                own.wait()
                own.link(v.tensor_tensor(out=goh, in0=over(iota[:, 0:NG], NT, 1),
                                         in1=i8[:, :, 0:1].to_broadcast([P, NT, NG]), op=ALU.is_equal))
                by_group = t32.rearrange("p t (e g) -> p t e g", g=NG)
                own.link(v.tensor_tensor(out=by_group, in0=sel.rearrange("p t (g e) -> p t e g", g=NG),
                                         in1=over(goh, EG, 2), op=ALU.mult))
                own.link(v.tensor_reduce(out=ing, in_=by_group, axis=AX, op=ALU.add))
                for t in range(NT):
                    own(v.max(out=m8[:, t], in_=ing[:, t]))
                own.wait()
                for t in range(NT):
                    own(v.max_index(out=i8[:, t], in_max=m8[:, t], in_values=ing[:, t]))
                own.wait()
                own.link(v.tensor_tensor(out=loh, in0=over(over(iota[:, 0:EG], 2, 1), NT, 1),
                                         in1=i8[:, :, 0:2].unsqueeze(3).to_broadcast([P, NT, 2, EG]), op=ALU.is_equal))
                own.link(v.tensor_tensor(out=pair, in0=loh[:, :, 0], in1=loh[:, :, 1], op=ALU.add))
                own.link(v.tensor_tensor(out=both.rearrange("p t (g e) -> p t g e", g=NG), in0=over(goh, EG, 3),
                                         in1=over(pair, NG, 2), op=ALU.mult))
                v.tensor_copy(both_b, both).then_inc(a_sb, 1)
                own.link(v.tensor_tensor(out=t32, in0=both, in1=scores, op=ALU.mult))
                own.link(v.tensor_reduce(out=gs, in_=t32, axis=AX, op=ALU.add))
                own.link(v.reciprocal(gs, gs))
                for t in range(NT):
                    own(v.tensor_scalar(out=gate[:, t, 0:NIT].rearrange("p (q e) -> p q e", e=NE),
                                        in0=over(t32[:, t], PASSES, 1), scalar1=gs[:, t:t + 1], scalar2=None,
                                        op0=ALU.mult))
                own.wait()
                dve.wait_ge(rank_ps, layer + 1)
                own(v.tensor_reduce(out=cnt, in_=psum[6][:, 2 * NE:3 * NE], axis=AX, op=ALU.max))
                own.link(v.scalar_tensor_tensor(out=t32, in0=psum[6][:, 0:2 * NE].rearrange("p (t e) -> p t e", t=NT),
                                                scalar=1.0, in1=both, op0=ALU.add, op1=ALU.mult))
                for q in range(PASSES):
                    own(v.tensor_scalar(out=pos[:, :, q * NE:(q + 1) * NE], in0=t32, scalar1=-1.0 - q * CAP,
                                        scalar2=None, op0=ALU.add))
                dve.wait_ge(init, 2)
                v.tensor_copy(flag[:, layer, 0:1], cnt).then_inc(flag_sb, 1)
                own.wait()

            def experts(s, steps, base):
                o2 = Own(dve, s.own)
                o2.n = s.o

                def picks(n, b):
                    for t in range(NT):
                        at = pos[:, t, bass.ds(n + base, 1)]
                        o2(v.tensor_scalar(out=pick[:, b, t], in0=k("iota"), scalar1=at, scalar2=None, op0=ALU.is_equal))
                        ins = v.tensor_scalar(out=gpick[:, b, t], in0=k("iota").unsqueeze(1).to_broadcast([P, 2, CAP]),
                                              scalar1=at, scalar2=gate[:, t, bass.ds(n + base, 1)],
                                              op0=ALU.is_equal, op1=ALU.mult)
                        o2(ins)
                    o2.wait()
                    dve.sem_inc(s.pick, 1)

                o2(v.memset(y_e, 0.0))
                o2.link(v.memset(gpT[:, 1], 0.0))
                dve.sem_inc(s.y, 1)
                dve.sem_inc(s.gpt, 1)
                picks(0, 0)
                dve.wait_ge(s.gathered, 1 + s.e)
                o2.link(v.tensor_copy(gpT[:, 0].rearrange("p t q -> p (t q)"), psum[5][:, 0:SEQ]))
                dve.sem_inc(s.gpt, 1)
                n0, per = o2.n, OWN_STEP
                assert n0 == s.o + OWN_HEAD

                def turn(i, ends):
                    for b in range(2):
                        n = i * 2 + b
                        o2.n, o2.loop = n0 + per * b, i * (2 * per)
                        if not (ends and b):
                            picks(n + 1, 1 - b)
                        dve.wait_ge(s.sig, n + (1 + s.e))
                        o2.link(v.scalar_tensor_tensor(out=hg, in0=eh, scalar=1.0, in1=psum[5][:, 0:SEQ], op0=ALU.add,
                                                       op1=ALU.mult))
                        v.scalar_tensor_tensor(out=hm.rearrange("p c q -> p q c"),
                                               in0=hg.rearrange("p (q c) -> p q c", c=2), scalar=0.5,
                                               in1=psum[5][:, SEQ:2 * SEQ].rearrange("p (q c) -> p q c", c=2),
                                               op0=ALU.mult, op1=ALU.mult).then_inc(s.hm, 1)
                        if not (ends and b):
                            dve.wait_ge(s.gathered, n + (2 + s.e))
                            o2.link(v.tensor_copy(gpT[:, 1 - b].rearrange("p t q -> p (t q)"), psum[5][:, 0:SEQ]))
                            dve.sem_inc(s.gpt, 1)
                        dve.wait_ge(s.y_ps, n + (1 + s.e))
                        o2.link(v.tensor_copy(y_e, psum[7][:]))
                        dve.sem_inc(s.y, 1)
                        assert o2.n == n0 + per * b + (OWN_LAST if ends and b else per)

                with dve.Fori(0, steps // 2 - 1) as i:
                    turn(i, False)
                turn(steps // 2 - 1, True)

            def moe(layer):
                route(layer)
                experts(fast[layer], NE, 0)
                dve.wait_ge(flag_sb, layer + 1)
                over = dve.value_load(flag[0:1, layer, 0:1])
                with dve.If(over > CAP):
                    dve.wait_ge(fast[layer].scattered, 1 + fast[layer].runs)
                    experts(more[layer], NIT - NE, NE)
                with dve.Else():
                    dve.nop()
                layer_norm(1 + 2 * layer)

            def gdn():
                dve.wait_ge(ba_ps, 1)
                dve.wait_ge(gdn_in, 80)
                hi = slice(32, 48)
                own.link(v.tensor_scalar(out=gT[hi, 0], in0=psum[3][hi, 0:SEQ], scalar1=ab[hi, 0:1], scalar2=None,
                                         op0=ALU.add))
                own.link(v.tensor_scalar(out=gT[hi, 1], in0=gT[hi, 0], scalar1=-1.0, scalar2=None, op0=ALU.mult))
                v.tensor_tensor(out=gT[hi, 1], in0=gT[hi, 0], in1=gT[hi, 1], op=ALU.min).then_inc(ba_ab, 1)
                dve.wait_ge(ba_exp, 2)
                own(v.tensor_scalar(out=ab[hi, 3:4], in0=ab[hi, 2:3], scalar1=-1.0, scalar2=None, op0=ALU.mult))
                own.link(v.tensor_scalar(out=gT[0:16, 2], in0=gT[0:16, 4], scalar1=1.0, scalar2=None, op0=ALU.add))
                own(v.reciprocal(gT[0:16, 2], gT[0:16, 2]))
                dve.wait_ge(ba_sp, 1)
                own.link(v.scalar_tensor_tensor(out=gT[hi, 0], in0=gT[hi, 0], scalar=0.0, in1=gT[hi, 1], op0=ALU.max,
                                                op1=ALU.add))
                own.link(v.tensor_scalar(out=gT[0:16, 3], in0=gT[hi, 0], scalar1=ab[hi, 3:4], scalar2=None, op0=ALU.mult))
                for c in range(NC_):
                    col = slice(c * C, (c + 1) * C)
                    own(v.tensor_tensor_scan(out=gcT[:, col], data0=k("ones")[0:16, 0:C], data1=gT[0:16, 3, col],
                                             initial=0.0, op0=ALU.mult, op1=ALU.add))
                own.wait()
                dve.sem_inc(gc_sb, 1)
                def decays(half, n):
                    h = 4 * half + n
                    dve.wait_ge(row_ps, h + 1)
                    if half:
                        dve.wait_ge(tl_ps, (LEVELS - 1) * 4)
                    bank = psum[ROW_BANKS[half] + n]
                    for c in range(NC_):
                        u = c * GH + h
                        own(v.scalar_tensor_tensor(out=ty[:, n, c], in0=bank[:, c * P:(c + 1) * P],
                                                   scalar=gcol[:, 0, u:u + 1], in1=k("decay_mask"),
                                                   op0=ALU.subtract, op1=ALU.add))
                    rowv = bank[:].rearrange("p (c e i) -> p c e i", c=NC_, e=2)
                    for e in range(2):
                        part = slice(e * C, (e + 1) * C)
                        own(v.tensor_tensor(out=gcol[part, 5].rearrange("p (c h) -> p c h", h=GH)[:, :, h],
                                            in0=rowv[part, :, e, C - 1],
                                            in1=gcol[part, 0].rearrange("p (c h) -> p c h", h=GH)[:, :, h],
                                            op=ALU.subtract))
                    own.wait()
                    dve.sem_inc(dm_sb, 1)

                dve.wait_ge(cw_sb, 1)
                for n in range(18):
                    if 1 <= n <= 16:
                        m = n - 1
                        b = m % 2
                        dve.wait_ge(ce_sb, m + 1)
                        if m < 8:
                            v.scalar_tensor_tensor(out=gq[:, m // 4, 2 * (m % 4):2 * (m % 4) + 2], in0=ce[:, b],
                                                   scalar=1.0, in1=cv[:, b], op0=ALU.add, op1=ALU.mult
                                                   ).then_inc(si_sb, 1)
                        else:
                            if m >= 10:
                                dve.wait_ge(vt_ps, m - 9)
                            for e in range(2):
                                own(v.scalar_tensor_tensor(out=vT[:, b, :, e], scalar=1.0,
                                                           in0=ce[:, b, e].rearrange("p (c i) -> p c i", c=NC_),
                                                           in1=cv[:, b, e].rearrange("p (c i) -> p c i", c=NC_),
                                                           op0=ALU.add, op1=ALU.mult))
                            own.wait()
                            dve.sem_inc(si_sb, 1)
                    if n < 16:
                        b = n % 2
                        dve.wait_ge(xc_sb, n + 1)
                        if n >= 2:
                            dve.wait_ge(si_sb, n - 1)
                        for tap in range(TAPS):
                            for i in range(2):
                                ch = 2 * n + i
                                wt = cw[:, tap * 32 + ch:tap * 32 + ch + 1]
                                src = xc[:, b, i, tap:tap + SEQ]
                                if tap == 0:
                                    own(v.tensor_scalar(out=cv[:, b, i], in0=src, scalar1=wt, scalar2=None, op0=ALU.mult))
                                else:
                                    own(v.scalar_tensor_tensor(out=cv[:, b, i], in0=src, scalar=wt, in1=cv[:, b, i],
                                                               op0=ALU.mult, op1=ALU.add))
                            own.wait()
                        dve.sem_inc(cv_sb, 1)
                    if 5 <= n < 13 and n % 2:
                        for m in (n - 5, n - 4):
                            dve.wait_ge(ss_sb, m + 1)
                            dst = gq[:, m // 4, 2 * (m % 4):2 * (m % 4) + 2]
                            v.scalar_tensor_tensor(out=dst, in0=dst, scalar=0.5, in1=rn[:, m % 2], op0=ALU.mult,
                                                   op1=ALU.mult).then_inc(qk_sb, 1)
                    if n == 11:
                        dve.wait_ge(qk_sb, 8)
                    if 11 <= n < 15:
                        decays(0, n - 11)
                    if n == 4:
                        dve.wait_ge(col_ps, 1)
                        own.link(v.tensor_copy(gcol[:, 0:2].rearrange("p w u -> p (w u)"), psum[3][:, 0:64]))
                        dve.sem_inc(col_sb, 1)
                    if n == 6:
                        dve.wait_ge(col_exp, 1)
                        own(v.tensor_scalar(out=gcol[:, 3], in0=gcol[:, 2], scalar1=GDN_SCALE, scalar2=None, op0=ALU.mult))
                        own(v.tensor_scalar(out=gcol[:, 4], in0=gcol[:, 2], scalar1=-1.0, scalar2=None, op0=ALU.mult))
                        own(v.tensor_scalar(out=gcol[:, 6], in0=gcol[:, 1], scalar1=-1.0, scalar2=None, op0=ALU.mult))
                        own.wait()
                for half in range(2):
                    if half:
                        dve.wait_ge(ao_sb, 16)

                    def decayed(n, w):
                        products = psum[4 + n][:].rearrange("p (c w i) -> p c w i", c=NC_, w=2)
                        for c in range(NC_):
                            u = c * GH + 4 * half + n
                            own(v.scalar_tensor_tensor(out=(att, nlt)[w][:, n, c].rearrange("p (e i) -> p e i", e=2),
                                                       in0=ty[:, n, c].rearrange("p (e i) -> p e i", e=2),
                                                       scalar=(GDN_SCALE, gcol[:, 6, u:u + 1])[w],
                                                       in1=products[:, c, w].unsqueeze(1).to_broadcast([P, 2, C]),
                                                       op0=ALU.mult, op1=ALU.mult))
                        own.wait()

                    for n in range(4):
                        h = 4 * half + n
                        dve.wait_ge(dt_sb, 2 * h + 2)
                        dve.wait_ge(kk_ps, h + 1)
                        decayed(n, 1)
                        dve.wait_ge(init, 7 + h)
                        v.copy_predicated(triT[:, n], levels[:, 0].unsqueeze(1).to_broadcast([P, NC_, P]),
                                          nlt[:, n]).then_inc(tri_init, 1)
                    dve.wait_ge(vt_ps, 8)
                    for n in range(4):
                        decayed(n, 0)
                        dve.sem_inc(att_sb, 1)
                    for lv in range(1, LEVELS):
                        for n in range(4):
                            dve.wait_ge(tl_ps, (half * (LEVELS - 1) + lv - 1) * 4 + n + 1)
                            dst = triT if lv == LEVELS - 1 else tri
                            v.copy_predicated(dst[:, n], levels[:, lv].unsqueeze(1).to_broadcast([P, NC_, P]),
                                              psum[4 + n][:].rearrange("p (c i) -> p c i", c=NC_)).then_inc(tri_sb, 1)
                    for n in range(0 if half else 4):
                        decays(1, n)
                    dve.wait_ge(dec_exp, half + 1)
                    own.link(v.memset(state, 0.0))
                    for g in range(18):
                        if g < 16 and g // 4:
                            c, n = g // 4, g % 4
                            u = c * GH + 4 * half + n
                            dve.wait_ge(ks_ps, half * 12 + g - 4 + 1)
                            if g >= 2:
                                dve.wait_ge(tr2_ps, half * 16 + g - 1)
                            v.scalar_tensor_tensor(out=rres[:, g % 2], in0=psum[g % 2][:, P:2 * P],
                                                   scalar=gcol[:, 4, u:u + 1], in1=vtok[:, c, 4 * half + n],
                                                   op0=ALU.mult, op1=ALU.add).then_inc(r_sb, 1)
                        elif g < 16:
                            dve.sem_inc(r_sb, 1)
                        if 1 <= g <= 16:
                            g1 = g - 1
                            c, n = g1 // 4, g1 % 4
                            u = c * GH + 4 * half + n
                            dve.wait_ge(vn_sb, half * 16 + g1 + 1)
                            if c < NC_ - 1:
                                if g1 >= 2:
                                    dve.wait_ge(su_ps, half * 12 + g1 - 1)
                                v.tensor_scalar(out=vdec[:, g1 % 2], in0=vnew[:, g1 % 2],
                                                scalar1=gcol[:, 5, u:u + 1], scalar2=None, op0=ALU.mult).then_inc(vd_sb, 1)
                            else:
                                dve.sem_inc(vd_sb, 1)
                        if g >= 2:
                            g2 = g - 2
                            G2 = half * 16 + g2
                            c, n = g2 // 4, g2 % 4
                            dve.wait_ge(ao_ps, G2 + 1)
                            dst = vtok[:, c, 4 * half + n]
                            if c:
                                dve.wait_ge(oq_sb, half * 12 + g2 - 4 + 1)
                                v.tensor_tensor(out=dst, in0=psum[4 + g2 % 2][:, 0:P], in1=oq[:, g2 % 2],
                                                op=ALU.add).then_inc(ao_sb, 1)
                            else:
                                v.tensor_copy(dst, psum[4 + g2 % 2][:, 0:P]).then_inc(ao_sb, 1)
                            if c < NC_ - 1:
                                dve.wait_ge(su_ps, half * 12 + g2 + 1)
                                for e in range(2):
                                    own(v.scalar_tensor_tensor(out=state[:, 2 * n + e], in0=state[:, 2 * n + e],
                                                               scalar=sdec[:, 4 * half + n, c, e:e + 1],
                                                               in1=psum[6 + e][:, 0:P], op0=ALU.mult, op1=ALU.add))
                                own.wait()
                                dve.sem_inc(st_sb, 1)
                dve.wait_ge(rms_sb, 1)
                for i in range(8):
                    zz, cp = i // 2, i % 2
                    z = zt[:, i % 4]
                    dve.wait_ge(z_exp, i + 1)
                    for cc in range(2):
                        for hh in range(2):
                            c, h = 2 * cp + cc, 2 * zz + hh
                            u = c * GH + h
                            own(v.scalar_tensor_tensor(out=vtok[:, c, h], in0=vtok[:, c, h], scalar=gcol[:, 7, u:u + 1],
                                                       in1=norm_g[:], op0=ALU.mult, op1=ALU.mult))
                    own.link(v.scalar_tensor_tensor(out=z, in0=z, scalar=1.0, in1=psum[Z_BANKS[i % 4]][:], op0=ALU.add,
                                                    op1=ALU.mult))
                    ot = vtok[:, 2 * cp:2 * cp + 2, 2 * zz:2 * zz + 2]
                    v.scalar_tensor_tensor(out=ot, in0=ot, scalar=0.5,
                                           in1=z.rearrange("p (c h d) -> p c h d", c=2, h=2), op0=ALU.mult,
                                           op1=ALU.mult).then_inc(og_sb, 1)
                layer_norm(2)

            attention()
            moe(0)
            gdn()
            moe(1)


_INPUTS = ("x", "ab_w_in", "ab_w_out", "gdn_w_in", "gdn_conv_w", "gdn_a_log", "gdn_dt_bias", "gdn_norm_g", "gdn_w_out",
           "mix_ln_g", "mix_ln_b", "router_w", "router_bias", "moe_w1", "moe_w3", "moe_w2", "ffn_ln_g", "ffn_ln_b")


def kernel(**inputs):
    import concourse.bacc as bacc
    from concourse.bass_utils import run_bass_kernel_spmd

    nc = bacc.Bacc("TRN2", target_bir_lowering=False, num_devices=1)
    const, levels = tables()
    arrays = {name: np.ascontiguousarray(inputs[name]) for name in _INPUTS}
    arrays["const"], arrays["levels"] = const, levels
    aps = {name: nc.dram_tensor(f"in_{name}", v.shape, mybir.dt.from_np(v.dtype), kind="ExternalInput").ap()
           for name, v in arrays.items()}
    out = nc.dram_tensor("out", (1, SEQ, D), F32, kind="ExternalOutput").ap()
    build(nc, aps, out)
    r = run_bass_kernel_spmd(nc, [{f"in_{name}": v for name, v in arrays.items()}], core_ids=[0])
    return r.results[0]["out"]
```
